# Optimizing a Trainium2 kernel written in Bass

```python
import math
import jax, jax.numpy as jnp
from jax import lax
import numpy as np

D_MODEL = 1024
BATCH = 1
SEQ = 256
DEPTH = 2
DEC_BATCH = 8
DEC_SEQ = 1
PAST_LEN = 1024
PAGE_SIZE = 128

HEAD_DIM = 64
D_MIX = D_MODEL
A_HEADS = 4
A_WIDTH = A_HEADS * HEAD_DIM
A_BRANCHES = ((128, 1), (512, 4), (2048, 16))
A_WIN = max(w for w, _ in A_BRANCHES)
B_HEADS = 8
B_KV_HEADS = 2
B_GROUP = B_HEADS // B_KV_HEADS
B_WIDTH = B_HEADS * HEAD_DIM
B_KV_WIDTH = B_KV_HEADS * HEAD_DIM
CMP_BLK = 32
SEL_BLK = 64
CMP_PER_SEL = SEL_BLK // CMP_BLK
N_SEL = 16
B_WIN = 512
FORCE_BONUS = 16.0
C_WIDTH = D_MIX - A_WIDTH - B_WIDTH
C_BLOCKS = 4
C_BLK = C_WIDTH // C_BLOCKS
CONV_W = 4
LRU_C = 8.0
D_FF = 2816
ALPHA = (2 * DEPTH) ** 0.25
BETA = (8 * DEPTH) ** -0.25
ROPE_THETA = 10000.0
Q_BLK = 128
EPS = 1e-5
SCALE = HEAD_DIM ** -0.5
IN_SPLITS = (A_WIDTH, A_WIDTH, A_WIDTH, B_WIDTH, B_KV_WIDTH, B_KV_WIDTH, B_KV_WIDTH, B_KV_WIDTH, B_KV_WIDTH, B_KV_WIDTH, 3 * B_HEADS, C_WIDTH, C_WIDTH)
IN_IS_VALUE = (0, 0, 1, 0, 0, 1, 0, 1, 0, 1, 0, 0, 0)
N_IN = sum(IN_SPLITS)

kernel_name = 'hybrid_dilated_nsa_rglru_step'

def layer_norm(x, g, b):
    xf = x.astype(jnp.float32)
    mu = jnp.mean(xf, -1, keepdims=True)
    var = jnp.mean(jnp.square(xf - mu), -1, keepdims=True)
    return ((xf - mu) * lax.rsqrt(var + EPS) * g + b).astype(x.dtype)

def rms_norm(x, g):
    xf = x.astype(jnp.float32)
    return (xf * lax.rsqrt(jnp.mean(jnp.square(xf), -1, keepdims=True) + EPS) * g).astype(x.dtype)

def swiglu(x, wg, wu, wd):
    return (jax.nn.silu(x @ wg) * (x @ wu)) @ wd

def rope(x, pos):
    half = HEAD_DIM // 2
    freq = ROPE_THETA ** (-jnp.arange(half, dtype=jnp.float32) / half)
    ang = pos.astype(jnp.float32)[:, None] * freq[None, :]
    cos = jnp.cos(ang)[:, None, :]
    sin = jnp.sin(ang)[:, None, :]
    x1 = x[..., :half].astype(jnp.float32)
    x2 = x[..., half:].astype(jnp.float32)
    return jnp.concatenate([x1 * cos - x2 * sin, x2 * cos + x1 * sin], -1).astype(x.dtype)

def masked_exp(s, mask):
    s = jnp.where(mask, s, -jnp.inf)
    m = jnp.max(s, axis=-1, keepdims=True)
    m = jnp.where(jnp.isfinite(m), m, 0.0)
    e = jnp.where(mask, jnp.exp(s - m), 0.0)
    return e, m, jnp.sum(e, axis=-1, keepdims=True)

def normalise(e, l):
    return e / jnp.where(l > 0, l, 1.0)

def q_slice(x, s):
    return lax.dynamic_slice_in_dim(x, s, Q_BLK, axis=1)

def over_query_blocks(fn, seq_len):
    out = lax.map(fn, jnp.arange(seq_len // Q_BLK, dtype=jnp.int32) * Q_BLK)
    out = jnp.moveaxis(out, 0, 1)
    return out.reshape((out.shape[0], seq_len) + out.shape[3:])

def dilated_attention(q, k_all, v_all, q_idx):
    outs, ms, ls = [], [], []
    for w, d in A_BRANCHES:
        offs = jnp.arange(w // d + 1, dtype=jnp.int32) * d
        idx = q_idx[:, None] - offs[None, :]
        valid = idx >= 0
        idx = jnp.maximum(idx, 0)
        kg = k_all[:, idx]
        vg = v_all[:, idx]
        s = jnp.einsum('bqhd,bqkhd->bqhk', q, kg).astype(jnp.float32) * SCALE
        e, m, l = masked_exp(s, valid[None, :, None, :])
        outs.append(jnp.einsum('bqhk,bqkhd->bqhd', e, vg.astype(jnp.float32)))
        ms.append(m)
        ls.append(l)
    m_all = jnp.stack(ms)
    wts = jnp.exp(m_all - jnp.max(m_all, 0, keepdims=True))
    num = jnp.sum(wts * jnp.stack(outs), 0)
    den = jnp.sum(wts * jnp.stack(ls), 0)
    return (num / den).astype(q.dtype)

def nsa_compress(kv_all, wk, wv):
    n_b, s_len = kv_all.shape[:2]
    nc = s_len // CMP_BLK
    blk = kv_all[:, :nc * CMP_BLK].reshape(n_b, nc, CMP_BLK, 2, B_KV_HEADS, HEAD_DIM)
    kc = jnp.einsum('bnjhd,jd->bnhd', blk[:, :, :, 0], wk)
    vc = jnp.einsum('bnjhd,jd->bnhd', blk[:, :, :, 1], wv)
    return kc, vc

def nsa_blocks(kv_all):
    n_b, s_len = kv_all.shape[:2]
    ns = -(-s_len // SEL_BLK)
    padded = jnp.pad(kv_all, ((0, 0), (0, ns * SEL_BLK - s_len), (0, 0), (0, 0), (0, 0)))
    blk = padded.reshape(n_b, ns, SEL_BLK, 2, B_KV_HEADS, HEAD_DIM)
    return blk[:, :, :, 0].transpose(0, 3, 1, 2, 4), blk[:, :, :, 1].transpose(0, 3, 1, 2, 4)

def nsa_attention(q, g, kcmp, vcmp, sel_k, sel_v, kw_pad, vw_pad, q_idx, w0):
    n_b, tq = q.shape[:2]
    nc = kcmp.shape[1]
    ns = sel_k.shape[2]
    ksel = min(N_SEL, ns)
    s_c = jnp.einsum('bqhgd,bnhd->bqhgn', q, kcmp).astype(jnp.float32) * SCALE
    vis = (jnp.arange(nc, dtype=jnp.int32) * CMP_BLK + CMP_BLK - 1)[None, :] <= q_idx[:, None]
    e, m, l = masked_exp(s_c, vis[None, :, None, None, :])
    p_c = normalise(e, l)
    o_c = jnp.einsum('bqhgn,bnhd->bqhgd', p_c, vcmp.astype(jnp.float32))
    imp = jnp.sum(p_c, 3)
    imp = jnp.pad(imp, ((0, 0), (0, 0), (0, 0), (0, ns * CMP_PER_SEL - nc)))
    imp = imp.reshape(n_b, tq, B_KV_HEADS, ns, CMP_PER_SEL).sum(-1)
    blk = jnp.arange(ns, dtype=jnp.int32)[None, :]
    cur = (q_idx // SEL_BLK)[:, None]
    forced = (blk == 0) | (blk == cur) | (blk == cur - 1)
    allowed = blk * SEL_BLK <= q_idx[:, None]
    score = jnp.where(allowed[None, :, None, :], imp + FORCE_BONUS * forced[None, :, None, :], -jnp.inf)
    top_s, top_i = lax.top_k(score, ksel)
    sel_ok = jnp.isfinite(top_s)
    gather = jax.vmap(jax.vmap(lambda kb, ix: kb[ix]))
    idx_t = top_i.transpose(0, 2, 1, 3)
    kg = gather(sel_k, idx_t)
    vg = gather(sel_v, idx_t)
    s_s = jnp.einsum('bqhgd,bhqnjd->bqhgnj', q, kg).astype(jnp.float32) * SCALE
    kpos = top_i[..., None] * SEL_BLK + jnp.arange(SEL_BLK, dtype=jnp.int32)
    ok = sel_ok[..., None] & (kpos <= q_idx[None, :, None, None, None])
    flat = ksel * SEL_BLK
    e, m, l = masked_exp(s_s.reshape(n_b, tq, B_KV_HEADS, B_GROUP, flat), ok.reshape(n_b, tq, B_KV_HEADS, 1, flat))
    p_s = normalise(e, l).reshape(s_s.shape)
    o_s = jnp.einsum('bqhgnj,bhqnjd->bqhgd', p_s, vg.astype(jnp.float32))
    band = B_WIN + tq
    kb = lax.dynamic_slice_in_dim(kw_pad, w0, band, axis=1)
    vb = lax.dynamic_slice_in_dim(vw_pad, w0, band, axis=1)
    kidx = w0 - B_WIN + jnp.arange(band, dtype=jnp.int32)
    qidx = w0 + jnp.arange(tq, dtype=jnp.int32)
    diff = qidx[:, None] - kidx[None, :]
    okw = (kidx[None, :] >= 0) & (diff >= 0) & (diff <= B_WIN)
    s_w = jnp.einsum('bqhgd,bkhd->bqhgk', q, kb).astype(jnp.float32) * SCALE
    e, m, l = masked_exp(s_w, okw[None, :, None, None, :])
    o_w = jnp.einsum('bqhgk,bkhd->bqhgd', normalise(e, l), vb.astype(jnp.float32))
    out = g[..., 0, None] * o_c + g[..., 1, None] * o_s + g[..., 2, None] * o_w
    return out.astype(q.dtype)

def rglru(xb, gb, prefix, h0, conv_w, conv_b, wr, br, wi, bi, lam):
    n_b, t = xb.shape[:2]
    xfull = jnp.concatenate([prefix.astype(xb.dtype), xb], axis=1)
    xc = conv_b
    for j in range(CONV_W):
        xc = xc + conv_w[j] * xfull[:, j:j + t]
    xr = xc.reshape(n_b, t, C_BLOCKS, C_BLK)
    r = jax.nn.sigmoid(jnp.einsum('btnc,ncd->btnd', xr, wr).reshape(n_b, t, C_WIDTH) + br)
    i = jax.nn.sigmoid(jnp.einsum('btnc,ncd->btnd', xr, wi).reshape(n_b, t, C_WIDTH) + bi)
    log_a = (-LRU_C * r.astype(jnp.float32)) * jax.nn.softplus(-lam.astype(jnp.float32))
    a = jnp.exp(log_a)
    u = jnp.sqrt(-jnp.expm1(2.0 * log_a)) * (i * xc).astype(jnp.float32)

    def step(h, au):
        h = au[0] * h + au[1]
        return h, h

    h_last, hs = lax.scan(step, h0.astype(jnp.float32), (a.swapaxes(0, 1), u.swapaxes(0, 1)))
    y = hs.swapaxes(0, 1).astype(xb.dtype) * jax.nn.gelu(gb)
    return y, h_last, xfull[:, xfull.shape[1] - (CONV_W - 1):]

def token_mixing(h, pos, lp, past):
    n_b, t, _ = h.shape
    offs = [int(v) for v in np.cumsum(IN_SPLITS)[:-1]]
    (aq, ak, av, bq, bck, bcv, bsk, bsv, bwk, bwv, bg, cx, cg) = jnp.split(h @ lp['w_in'], offs, axis=-1)
    heads = lambda z, n: z.reshape(n_b, t, n, HEAD_DIM)
    qa = rope(heads(aq, A_HEADS), pos)
    kva_new = jnp.stack([rope(heads(ak, A_HEADS), pos), heads(av, A_HEADS)], 2)
    qb = rope(heads(bq, B_HEADS), pos).reshape(n_b, t, B_KV_HEADS, B_GROUP, HEAD_DIM)
    kvc_new = jnp.stack([rope(heads(bck, B_KV_HEADS), pos), heads(bcv, B_KV_HEADS)], 2)
    kvs_new = jnp.stack([rope(heads(bsk, B_KV_HEADS), pos), heads(bsv, B_KV_HEADS)], 2)
    kvw_new = jnp.stack([rope(heads(bwk, B_KV_HEADS), pos), heads(bwv, B_KV_HEADS)], 2)
    gates = jax.nn.sigmoid((bg + lp['b_gate']).astype(jnp.float32)).reshape(n_b, t, B_KV_HEADS, B_GROUP, 3)
    if past is None:
        kva_all, a_off = kva_new, 0
        kvc_all, kvs_all, b_off = kvc_new, kvs_new, 0
        kvw_all, w_off = kvw_new, 0
        prefix = jnp.zeros((n_b, CONV_W - 1, C_WIDTH), h.dtype)
        h0 = jnp.zeros((n_b, C_WIDTH), jnp.float32)
    else:
        pt = past['page_table']

        def from_pages(pool):
            gp = pool[pt]
            return gp.reshape((gp.shape[0], gp.shape[1] * gp.shape[2]) + gp.shape[3:])

        a_off = past['a'].shape[1]
        kva_all = jnp.concatenate([past['a'], kva_new], 1)
        b_off = pt.shape[1] * PAGE_SIZE
        kvc_all = jnp.concatenate([from_pages(past['bc']), kvc_new], 1)
        kvs_all = jnp.concatenate([from_pages(past['bs']), kvs_new], 1)
        w_off = past['bw'].shape[1]
        kvw_all = jnp.concatenate([past['bw'], kvw_new], 1)
        prefix, h0 = past['conv'], past['h']
    ka_all, va_all = kva_all[:, :, 0], kva_all[:, :, 1]
    kcmp, vcmp = nsa_compress(kvc_all, lp['cmp_wk'], lp['cmp_wv'])
    sel_k, sel_v = nsa_blocks(kvs_all)
    pad_w = ((0, 0), (B_WIN, 0), (0, 0), (0, 0))
    kw_pad = jnp.pad(kvw_all[:, :, 0], pad_w)
    vw_pad = jnp.pad(kvw_all[:, :, 1], pad_w)
    ar_q = jnp.arange(Q_BLK, dtype=jnp.int32)
    if past is None:
        ya = over_query_blocks(lambda s: dilated_attention(q_slice(qa, s), ka_all, va_all, s + ar_q), t)
        yb = over_query_blocks(lambda s: nsa_attention(q_slice(qb, s), q_slice(gates, s), kcmp, vcmp, sel_k, sel_v, kw_pad, vw_pad, s + ar_q, s), t)
    else:
        ar_t = jnp.arange(t, dtype=jnp.int32)
        ya = dilated_attention(qa, ka_all, va_all, a_off + ar_t)
        yb = nsa_attention(qb, gates, kcmp, vcmp, sel_k, sel_v, kw_pad, vw_pad, b_off + ar_t, w_off)
    yc, h_last, conv_new = rglru(cx, cg, prefix, h0, lp['conv_w'], lp['conv_b'], lp['lru_wr'], lp['lru_br'], lp['lru_wi'], lp['lru_bi'], lp['lru_lam'])
    y = jnp.concatenate([rms_norm(ya.reshape(n_b, t, A_WIDTH), lp['out_g_a']), rms_norm(yb.reshape(n_b, t, B_WIDTH), lp['out_g_b']), rms_norm(yc, lp['out_g_c'])], -1) @ lp['w_out']
    if past is None:
        new_a = kva_new[:, t - min(A_WIN, t):]
        page_shape = (n_b, t // PAGE_SIZE, PAGE_SIZE, 2, B_KV_HEADS, HEAD_DIM)
        new_bc = kvc_new.reshape(page_shape)
        new_bs = kvs_new.reshape(page_shape)
        new_bw = kvw_new[:, t - min(B_WIN, t):]
    else:
        new_a, new_bc, new_bs, new_bw = kva_new, kvc_new, kvs_new, kvw_new
    return y, (new_a, new_bc, new_bs, new_bw, h_last.astype(h.dtype), conv_new)

def decoder_layer(x, pos, lp, past):
    x = layer_norm(ALPHA * x + 0.5 * swiglu(x, lp['ffn_wg'][0], lp['ffn_wu'][0], lp['ffn_wd'][0]), lp['ln_g'][0], lp['ln_b'][0])
    y, st = token_mixing(x, pos, lp, past)
    x = layer_norm(ALPHA * x + y, lp['ln_g'][1], lp['ln_b'][1])
    x = layer_norm(ALPHA * x + 0.5 * swiglu(x, lp['ffn_wg'][1], lp['ffn_wu'][1], lp['ffn_wd'][1]), lp['ln_g'][2], lp['ln_b'][2])
    return x, st

def setup_inputs(seed: int = 0) -> dict:
    key = jax.random.key(seed)
    ks = jax.random.split(key, 32)
    f32 = jnp.float32
    nrm = lambda k, shape, s=1.0: jax.random.normal(k, shape, f32) * s
    n_pages = PAST_LEN // PAGE_SIZE
    n_used = DEC_BATCH * n_pages
    n_pool = n_used + n_used // 4
    a_buf = min(A_WIN, PAST_LEN)
    w_buf = min(B_WIN, PAST_LEN)
    col_scale = jnp.concatenate([jnp.full((n,), BETA if v else 1.0, f32) for n, v in zip(IN_SPLITS, IN_IS_VALUE)])
    a0 = jax.random.uniform(ks[21], (DEPTH, C_WIDTH), f32, 0.9, 0.999)
    a_root = a0 ** (1.0 / LRU_C)
    return {
        'x_prompt': nrm(ks[0], (BATCH, SEQ, D_MODEL)),
        'x_sample': nrm(ks[1], (DEC_BATCH, DEC_SEQ, D_MODEL)),
        'cache_a_kv': nrm(ks[2], (DEPTH, DEC_BATCH, a_buf, 2, A_HEADS, HEAD_DIM)),
        'cache_bc_kv': nrm(ks[3], (DEPTH, n_pool, PAGE_SIZE, 2, B_KV_HEADS, HEAD_DIM)),
        'cache_bs_kv': nrm(ks[4], (DEPTH, n_pool, PAGE_SIZE, 2, B_KV_HEADS, HEAD_DIM)),
        'cache_bw_kv': nrm(ks[5], (DEPTH, DEC_BATCH, w_buf, 2, B_KV_HEADS, HEAD_DIM)),
        'state_c_h': nrm(ks[6], (DEPTH, DEC_BATCH, C_WIDTH), 0.5),
        'state_c_conv': nrm(ks[7], (DEPTH, DEC_BATCH, CONV_W - 1, C_WIDTH)),
        'page_table': jax.random.permutation(ks[8], n_pool)[:n_used].reshape(DEC_BATCH, n_pages).astype(jnp.int32),
        'w_in': nrm(ks[9], (DEPTH, D_MODEL, N_IN), D_MODEL ** -0.5) * col_scale,
        'b_gate': nrm(ks[10], (DEPTH, 3 * B_HEADS), 0.01),
        'cmp_wk': (1.0 + nrm(ks[11], (DEPTH, CMP_BLK, HEAD_DIM), 0.1)) / CMP_BLK,
        'cmp_wv': (1.0 + nrm(ks[12], (DEPTH, CMP_BLK, HEAD_DIM), 0.1)) / CMP_BLK,
        'out_g_a': 1.0 + nrm(ks[13], (DEPTH, A_WIDTH), 0.1),
        'out_g_b': 1.0 + nrm(ks[14], (DEPTH, B_WIDTH), 0.1),
        'out_g_c': 1.0 + nrm(ks[15], (DEPTH, C_WIDTH), 0.1),
        'conv_w': nrm(ks[16], (DEPTH, CONV_W, C_WIDTH), CONV_W ** -0.5),
        'conv_b': nrm(ks[17], (DEPTH, C_WIDTH), 0.01),
        'lru_wr': nrm(ks[18], (DEPTH, C_BLOCKS, C_BLK, C_BLK), C_BLK ** -0.5),
        'lru_br': nrm(ks[19], (DEPTH, C_WIDTH), 0.01),
        'lru_wi': nrm(ks[20], (DEPTH, C_BLOCKS, C_BLK, C_BLK), C_BLK ** -0.5),
        'lru_bi': nrm(ks[22], (DEPTH, C_WIDTH), 0.01),
        'lru_lam': jnp.log(a_root) - jnp.log1p(-a_root),
        'w_out': nrm(ks[23], (DEPTH, D_MIX, D_MODEL), D_MIX ** -0.5 * BETA),
        'ln_g': 1.0 + nrm(ks[24], (DEPTH, 3, D_MODEL), 0.1),
        'ln_b': nrm(ks[25], (DEPTH, 3, D_MODEL), 0.01),
        'ffn_wg': nrm(ks[26], (DEPTH, 2, D_MODEL, D_FF), D_MODEL ** -0.5),
        'ffn_wu': nrm(ks[27], (DEPTH, 2, D_MODEL, D_FF), D_MODEL ** -0.5),
        'ffn_wd': nrm(ks[28], (DEPTH, 2, D_FF, D_MODEL), D_FF ** -0.5 * BETA),
    }

def reference(x_prompt, x_sample, cache_a_kv, cache_bc_kv, cache_bs_kv, cache_bw_kv, state_c_h, state_c_conv, page_table, w_in, b_gate, cmp_wk, cmp_wv, out_g_a, out_g_b, out_g_c, conv_w, conv_b, lru_wr, lru_br, lru_wi, lru_bi, lru_lam, w_out, ln_g, ln_b, ffn_wg, ffn_wu, ffn_wd):
    pos_p = jnp.arange(x_prompt.shape[1], dtype=jnp.int32)
    past_len = page_table.shape[1] * PAGE_SIZE
    pos_s = past_len + jnp.arange(x_sample.shape[1], dtype=jnp.int32)
    hp, hs = x_prompt, x_sample
    new_p, new_s = [], []
    for l in range(DEPTH):
        lp = {'w_in': w_in[l], 'b_gate': b_gate[l], 'cmp_wk': cmp_wk[l], 'cmp_wv': cmp_wv[l],
              'out_g_a': out_g_a[l], 'out_g_b': out_g_b[l], 'out_g_c': out_g_c[l],
              'conv_w': conv_w[l], 'conv_b': conv_b[l], 'lru_wr': lru_wr[l], 'lru_br': lru_br[l],
              'lru_wi': lru_wi[l], 'lru_bi': lru_bi[l], 'lru_lam': lru_lam[l], 'w_out': w_out[l],
              'ln_g': ln_g[l], 'ln_b': ln_b[l], 'ffn_wg': ffn_wg[l], 'ffn_wu': ffn_wu[l], 'ffn_wd': ffn_wd[l]}
        past = {'a': cache_a_kv[l], 'bc': cache_bc_kv[l], 'bs': cache_bs_kv[l], 'bw': cache_bw_kv[l],
                'h': state_c_h[l], 'conv': state_c_conv[l], 'page_table': page_table}
        hp, st_p = decoder_layer(hp, pos_p, lp, None)
        hs, st_s = decoder_layer(hs, pos_s, lp, past)
        new_p.append(st_p)
        new_s.append(st_s)
    a_p, bc_p, bs_p, bw_p, h_p, conv_p = [jnp.stack(z) for z in zip(*new_p)]
    a_s, bc_s, bs_s, bw_s, h_s, conv_s = [jnp.stack(z) for z in zip(*new_s)]
    return (hp, hs, a_p, a_s, bc_p, bc_s, bs_p, bs_s, bw_p, bw_s, h_p, h_s, conv_p, conv_s)


_drawn_inputs = setup_inputs


def setup_inputs(seed=0):
    import zlib

    import numpy as np

    out = dict(_drawn_inputs(seed))
    spreads = {}
    factors = {'b_gate': 23.259, 'cmp_wk': 16.187, 'lru_br': 29.833, 'lru_bi': 8.0}
    for name, (base, spread) in spreads.items():
        noise = np.random.default_rng([zlib.crc32(name.encode()), seed]).standard_normal(out[name].shape)
        drawn = base * np.exp(spread * noise) if base else spread * noise
        out[name] = __import__('jax').numpy.asarray(drawn.astype(out[name].dtype))
    for name, factor in factors.items():
        out[name] = (out[name] * factor).astype(out[name].dtype)
    return out
```

```python
from contextlib import ExitStack

import concourse.bass as bass
from concourse import mybir

P = 128
D_MODEL = 1024
SEQ = 256
DEPTH = 2
DEC = 8
PAST = 1024
PAGE = 128
PAGES = PAST // PAGE
HD = 64
D_FF = 2816
CMP = 32
C_WIDTH = 256
ALPHA = (2 * DEPTH) ** 0.25
EPS = 1e-5
SCALE = HD ** -0.5
LRU_C = 8.0
MASKED = -1e30

TOK = SEQ + DEC
KC = D_MODEL // P
FC = D_FF // P
TT = SEQ // P
N_TOKEN_MAJOR = 2048
N_GATES = 24
C_COL = N_TOKEN_MAJOR + N_GATES

AQ, AK, AV, BQ, BC, BS, BW = 0, 256, 512, 768, 1280, 1536, 1792

SLOTS = 3
SLOT = 4096
GROUP = 256
FFN_GROUPS = D_FF // GROUP
FFN_USES = FFN_GROUPS + KC
MIX_USES = 5 + 2
LAYER_USES = 2 * FFN_USES + MIX_USES
assert LAYER_USES % SLOTS == 0
WIN_USE, WOUT_USE = FFN_USES, FFN_USES + 5
LOOPED = FFN_GROUPS // SLOTS

HALF = DEC // 2
RING = HALF
RING_W = PAGES * 256 + 4 * 256 + 2 * 512
RB, RA = HALF * 8, HALF * 4
N_SEL = PAST + 1
N_WIN = 512 + 1
N_A = 256 + 1

ALU = mybir.AluOpType
ACT = mybir.ActivationFunctionType
F32 = mybir.dt.float32
I32 = mybir.dt.int32
AX_X = mybir.AxisListType.X

V_START = KC + DEPTH
V_LAYER = 12 + 3 + 2 + 1 + 1 + 2 * (2 * HALF + 1 + 1 + 2)
A_LAYER = 2 + 10 + 4 + 2 * (1 + 10) + 2 * 2 * HALF

TABLE = {}
TABLE_COLS = 0
for _name, _cols in (("ident", P), ("mean", P), ("mask_a", 2 * SEQ), ("mask_c", 2 * SEQ), ("vis_add", 16),
                     ("vis", 16), ("cos", 3 * HD), ("sin", 3 * HD), ("sel4", 4), ("selw", 60), ("selrep", 2 * HD),
                     ("log_a", N_A), ("same", RB), ("expand", 2 * RB), ("headmask", N_GATES),
                     ("index", 14), ("own", 16), ("own_a", 16), ("maskv", 512)):
    TABLE[_name] = (TABLE_COLS, TABLE_COLS + _cols)
    TABLE_COLS += _cols


def landed_counts():
    dmas = [2] * LAYER_USES
    dmas[WOUT_USE] = dmas[WOUT_USE + 1] = 4
    total, out = [0] * SLOTS, []
    for k, n in enumerate(dmas):
        total[k % SLOTS] += 16 * n
        out.append(total[k % SLOTS])
    return out, total


class Tally:

    def __init__(self):
        self.n = {}

    def next(self, sem, by=1):
        self.n[sem] = self.n.get(sem, 0) + by
        return self.n[sem]

    def now(self, sem):
        return self.n.get(sem, 0)


def build(nc, x_prompt, x_sample, cache_a_kv, cache_bc_kv, cache_bs_kv, cache_bw_kv, state_c_h, state_c_conv,
          page_table, w_in, b_gate, cmp_wk, cmp_wv, out_g_a, out_g_b, out_g_c, conv_w, conv_b, lru_wr, lru_br,
          lru_wi, lru_bi, lru_lam, w_out, ln_g, ln_b, ffn_wg, ffn_wu, ffn_wd, table,
          y_prompt, y_sample, a_prompt, a_sample, bc_prompt, bc_sample, bs_prompt, bs_sample, bw_prompt, bw_sample,
          h_prompt, h_sample, conv_prompt, conv_sample):
    n_pool = cache_bc_kv.shape[1]
    ctx = ExitStack()
    with ctx:
        def sb(name, shape, dt=F32):
            return ctx.enter_context(nc.sbuf_tensor(name, shape, dt))

        names = {}

        def sem(name):
            return ctx.enter_context(nc.semaphore(name))

        consts = sb("consts", [P, TABLE_COLS])
        weights = sb("weights", [P, SLOTS, SLOT])
        ring = sb("ring", [P, RING, RING_W])
        x = sb("x", [P, KC, TOK])
        z = sb("z", [P, KC, TOK])
        bc_pages = sb("bc_pages", [P, 2, 4, 256])
        params = sb("params", [P, DEPTH, 72])
        states = sb("states", [P, DEPTH, 64])
        cmp_w = sb("cmp_w", [P, DEPTH, 256])
        gate_bias = sb("gate_bias", [P, DEPTH, N_GATES])
        gate_w = sb("gate_w", [P, KC, N_GATES])
        lru_w = sb("lru_w", [P, 4, P])
        decay = sb("decay", [P, DEPTH, 2])
        eps = sb("eps", [P, 2])
        mean_sb = sb("mean_sb", [P, TOK])
        rstd = sb("rstd", [P, 3, TOK])
        pt_sb = sb("pt_sb", [1, DEC * PAGES], I32)
        shared = sb("shared", [P, 12560])
        at = [0]

        def carve(cols, reset=None):
            if reset is not None:
                at[0] = reset
            a = at[0]
            at[0] += cols
            assert at[0] <= 12560, at[0]
            return shared[:, a:a + cols]

        hidden = carve(FC * TOK, 0).rearrange("p (c t) -> p c t", c=FC)
        silu = carve(2 * TOK).rearrange("p (c t) -> p c t", c=2)
        tokens = carve(TT * 2048, 0).rearrange("p (t n) -> p t n", t=TT)
        feats = carve(10 * TOK).rearrange("p (c t) -> p c t", c=10)
        mixed = carve(KC * TOK).rearrange("p (c t) -> p c t", c=KC)
        squares = carve(2 * TOK).rearrange("p (c t) -> p c t", c=2)
        gates = carve(3 * N_GATES).rearrange("p (t n) -> p t n", t=3)
        scratch = at[0]
        rope_t = carve(2 * 512).rearrange("p (t n) -> p t n", t=2)
        conv_x = carve(2 * 260).rearrange("p (c t) -> p c t", c=2)
        conv_s = carve(2 * DEC * 4).rearrange("p (c b j) -> p c b j", c=2, b=DEC)
        gelu = carve(2 * TOK).rearrange("p (c t) -> p c t", c=2)
        lru_i = carve(2 * TOK, scratch).rearrange("p (c t) -> p c t", c=2)
        xc, lru_r, lru_t = mixed[:, 0:2, :], mixed[:, 2:4, :], mixed[:, 4:6, :]
        probs = carve(3 * 512, scratch).rearrange("p (r b n) -> p r b n", r=3, b=2)
        probs_t = carve(2 * 512).rearrange("p (r n) -> p r n", r=2)
        prod_c = probs_t
        stat = carve(4 * 8).rearrange("p (r n) -> p r n", r=4)
        finals = carve(72).rearrange("p (c t) -> p c t", c=2)
        finals_t = carve(256)
        vcmp = squares[:, :, :].rearrange("p c t -> p (c t)")[:, 0:512]
        pc_t, pc, kcmp, pc_stat = mean_sb[:, 0:128], mean_sb[:, 128:192], mean_sb[:, 192:200], mean_sb[:, 200:224]
        key_t = carve(4 * 512, 0).rearrange("p (e n) -> p e n", e=4)
        kcmp_s = carve(P)
        vcmp_s = carve(512)
        s_sel = carve(N_SEL)
        s_cmp = carve(CMP)
        s_a = carve(N_A)
        s_stat = carve(96)
        own_p = carve(24)[:, :]
        q_b = carve(160, scratch)
        q_a = carve(144)
        s_win = carve(N_WIN)
        p_t = carve(544)
        stage = carve(3 * D_MODEL, 0).rearrange("p (t n) -> p t n", t=3)
        rows = carve(2 * DEPTH * P).rearrange("p (l n) -> p l n", l=2 * DEPTH)
        z_flat = z[:, :, :].rearrange("p c t -> p (c t)")
        samples = z_flat[0:DEC, 0:2048]

        def table_of(name, rows_=P):
            a, b = TABLE[name]
            return consts[0:rows_, a:b]

        ident = table_of("ident")
        mean_w = table_of("mean")

        def slot(k):
            return weights[:, k % SLOTS, :]

        def rows_of(t):
            if t < TT:
                return P, slice(t * P, (t + 1) * P), tokens[:, t, :]
            return DEC, slice(SEQ, TOK), samples

        banks = [ctx.enter_context(nc.psum_tensor(f"bank{i}", [P, 512], F32)) for i in range(8)]

        consts_in, x_in, rows_in, page_in = sem("consts_in"), sem("x_in"), sem("rows_in"), sem("page_in")
        small_in, gate_w_in, lru_w_in = sem("small_in"), sem("gate_w_in"), sem("lru_w_in")
        landed = [sem(f"landed{i}") for i in range(SLOTS)]
        ring_in = [sem(f"ring_in{i}") for i in range(RING)]
        ring_used = sem("ring_used")
        bc_in = [sem(f"bc_in{i}") for i in range(2)]
        bc_weighted, bc_used = sem("bc_weighted"), sem("bc_used")
        cleared = sem("cleared")
        v_full, v_free = sem("v_full"), sem("v_free")
        a_full, a_free = sem("a_full"), sem("a_free")
        s_full, s_free = sem("s_full"), sem("s_free")
        gate_full, up_full, silu_done, hidden_done = sem("gate_full"), sem("up_full"), sem("silu_done"), sem("hidden_done")
        y_full, z_done, sq_done, stat_done = sem("y_full"), sem("z_done"), sem("sq_done"), sem("stat_done")
        var_done, std_done, norm_done, x_ready = sem("var_done"), sem("std_done"), sem("norm_done"), sem("x_ready")
        tok_ready, gates_raw, gates_ready = sem("tok_ready"), sem("gates_raw"), sem("gates_ready")
        xc_ready, gate_r, lru_f, lru_s, gelu_ready, finals_ready = (
            sem("xc_ready"), sem("lru_gates"), sem("lru_f"), sem("lru_s"), sem("gelu_ready"), sem("finals_ready"))
        prod_ready, cmp_ready, masked, exps, probs_ready, pv_done = (
            sem("prod_ready"), sem("cmp_ready"), sem("masked"), sem("exps"), sem("probs_ready"), sem("pv_done"))
        mix_ready = sem("mix_ready")
        q_ready, cmp_full, cmp_out = sem("q_ready"), sem("cmp_full"), sem("cmp_out")
        kt_used = sem("kt_used")
        s_masked, s_exps, imp_ready, s_probs, s_pt = (
            sem("s_masked"), sem("s_exps"), sem("imp_ready"), sem("s_probs"), sem("s_pt"))
        rms_sq, rms_stat, rms_var, rms_std, yn_ready = sem("rms_sq"), sem("rms_stat"), sem("rms_var"), sem("rms_std"), sem("yn_ready")
        vec, act_own = sem("vector_step"), sem("scalar_step")
        stage_ready, rows_stored, states_stored, y_stored = (
            sem("stage_ready"), sem("rows_stored"), sem("states_stored"), sem("y_stored"))
        state_ready = sem("state_ready")

        landed_at, landed_layer = landed_counts()

        def landed_value(l, k):
            return l * landed_layer[k % SLOTS] + landed_at[k]

        block = ctx.enter_context(nc.Block())

        @block.sync
        def _(sp):
            bc_count, ring_count = [0], [0]
            sp.dma_start(pt_sb[:, :], page_table.rearrange("b p -> (b p)").unsqueeze(0)).then_inc(page_in, 16)
            sp.dma_start(stage[:, 0:TT, :], x_prompt[0].rearrange("(t p) d -> p t d", p=P)).then_inc(x_in, 16)
            sp.dma_start(stage[0:DEC, TT, :], x_sample.rearrange("b s d -> (b s) d")).then_inc(x_in, 16)
            sp.dma_start(consts[:, :], table).then_inc(consts_in, 16)
            sp.wait_ge(page_in, 16)

            def used(l, k):
                if k < 0:
                    l, k = l - 1, k + LAYER_USES
                if WIN_USE <= k < WIN_USE + 4:
                    return v_full, V_START + l * V_LAYER + 3 * (k - WIN_USE + 1)
                if k == WIN_USE + 4:
                    return a_full, l * A_LAYER + 2
                if k in (WOUT_USE, WOUT_USE + 1):
                    return y_full, (3 * l + 1) * KC + 4 * (k - WOUT_USE + 1)
                j = k > WOUT_USE
                g = k - (WOUT_USE + 2) * j
                if g < FFN_GROUPS:
                    return up_full, (2 * l + j) * FC + 2 * (g + 1)
                return y_full, (3 * l + 2 * j) * KC + g - FFN_GROUPS + 1

            def load_slot(l, k, parts):
                if l * LAYER_USES + k >= SLOTS:
                    sp.wait_ge(*used(l, k - SLOTS))
                for dst, src in parts:
                    sp.dma_start(dst, src).then_inc(landed[k % SLOTS], 16)

            def ffn_parts(l, j, k, col):
                dst = slot(k).rearrange("p (w c f) -> p w c f", w=2, c=KC)
                return [(dst[:, i, :, :], w[l, j].rearrange("(c p) f -> p c f", p=P)[:, :, col])
                        for i, w in enumerate((ffn_wg, ffn_wu))]

            def load_ring(l, b):
                n = ring_count[0]
                s = n % RING
                ring_count[0] += 1
                if n >= RING:
                    sp.wait_ge(ring_used, n - RING + 1)
                for p in range(PAGES):
                    page = sp.value_load(pt_sb[0:1, b * PAGES + p:b * PAGES + p + 1], min_val=0, max_val=n_pool - 1)
                    sp.dma_start(ring[:, s, p * 256:(p + 1) * 256],
                                 cache_bs_kv[l, bass.ds(page, 1)].rearrange("o r a h d -> (o r) (a h d)"))\
                        .then_inc(ring_in[s], 16)
                sp.dma_start(ring[:, s, 2048:3072].rearrange("p (t n) -> p t n", t=4),
                             cache_bw_kv[l, b].rearrange("(t p) a h d -> p t (a h d)", p=P)).then_inc(ring_in[s], 16)
                rows_a = cache_a_kv[l, b].rearrange("r a h d -> r (a h d)")
                sp.dma_start(ring[:, s, 3072:3584], rows_a[PAST - P:PAST, :]).then_inc(ring_in[s], 16)
                sp.dma_start(ring[0:96, s, 3584:4096],
                             rows_a[512:896, :].rearrange("(p s) n -> p s n", s=4)[:, 0, :]).then_inc(ring_in[s], 16)
                sp.dma_start(ring[96:P, s, 3584:4096],
                             rows_a[0:512, :].rearrange("(p s) n -> p s n", s=16)[:, 0, :]).then_inc(ring_in[s], 16)

            def load_bc(l, b, part):
                n = bc_count[0]
                bc_count[0] += 1
                if n >= 2:
                    sp.wait_ge(bc_used, n - 1)
                for i in range(4):
                    p = part * 4 + i
                    page = sp.value_load(pt_sb[0:1, b * PAGES + p:b * PAGES + p + 1], min_val=0, max_val=n_pool - 1)
                    sp.dma_start(bc_pages[:, n % 2, i, :],
                                 cache_bc_kv[l, bass.ds(page, 1)].rearrange("o r a h d -> (o r) (a h d)"))\
                        .then_inc(bc_in[n % 2], 16)

            def ffn(l, j, base, extra):
                first = 2 if extra else 1
                for g in range(first * SLOTS):
                    load_slot(l, base + g, ffn_parts(l, j, base + g, slice(g * GROUP, (g + 1) * GROUP)))
                    if extra:
                        extra(g)
                with sp.Fori(first, LOOPED) as i:
                    for s in range(SLOTS):
                        sp.wait_ge(up_full, (2 * l + j) * FC + 2 * (s - SLOTS + 1) + i * (2 * SLOTS))
                        for dst, src in ffn_parts(l, j, base + s, bass.ds(i * (SLOTS * GROUP) + s * GROUP, GROUP)):
                            sp.dma_start(dst, src).then_inc(landed[(base + s) % SLOTS], 16)
                for g in range(LOOPED * SLOTS, FFN_GROUPS):
                    load_slot(l, base + g, ffn_parts(l, j, base + g, slice(g * GROUP, (g + 1) * GROUP)))
                wd = ffn_wd[l, j].rearrange("(c p) d -> p c d", p=P)
                for g in range(KC):
                    k = base + FFN_GROUPS + g
                    dst = slot(k)[:, 0:FC * P].rearrange("p (c d) -> p c d", c=FC)
                    load_slot(l, k, [(dst[:, a:a + FC // 2, :], wd[:, a:a + FC // 2, g * P:(g + 1) * P])
                                     for a in (0, FC // 2)])

            for l in range(DEPTH):
                def behind(g, l=l):
                    if g < HALF:
                        load_ring(l, g)

                ffn(l, 0, 0, behind)
                load_bc(l, 0, 0)
                load_bc(l, 0, 1)
                w = w_in[l].rearrange("(c p) n -> p c n", p=P)
                if l:
                    sp.wait_ge(v_full, V_START + (l - 1) * V_LAYER + 15)
                sp.dma_start(gate_w[:, :, :], w[:, :, N_TOKEN_MAJOR:C_COL]).then_inc(gate_w_in, 16)
                for g in range(5):
                    col = slice(g * 512, (g + 1) * 512) if g < 4 else slice(C_COL, C_COL + 512)
                    dst = slot(WIN_USE + g).rearrange("p (c n) -> p c n", c=KC)
                    load_slot(l, WIN_USE + g, [(dst[:, a:a + 4, :], w[:, a:a + 4, col]) for a in (0, 4)])
                for b in range(HALF):
                    for part in range(2):
                        if b or part > 1:
                            load_bc(l, b, part)
                wo = w_out[l]
                for g in range(2):
                    dst = slot(WOUT_USE + g).rearrange("p (c n) -> p c n", c=KC)
                    col = slice(g * 512, (g + 1) * 512)
                    rows_b = wo[256:768, col].rearrange("(k g d) n -> k d g n", k=2, g=4)
                    load_slot(l, WOUT_USE + g, [
                        (dst[:, 0:2, :], wo[0:256, col].rearrange("(c p) n -> p c n", p=P)),
                        (dst[0:HD, 2:6, :], rows_b[0]), (dst[HD:P, 2:6, :], rows_b[1]),
                        (dst[:, 6:8, :], wo[768:1024, col].rearrange("(c p) n -> p c n", p=P))])
                for b in range(HALF, DEC):
                    load_ring(l, b)
                for b in range(HALF, DEC):
                    for part in range(2):
                        load_bc(l, b, part)
                ffn(l, 1, WOUT_USE + 2, None)

        @block.gpsimd
        def _(pool):
            pool.memset(lru_w[:, :, :], 0.0).then_inc(cleared, 1)
            seen = Tally()
            for l in range(DEPTH):
                r0, r1 = rows[:, 2 * l, :], rows[:, 2 * l + 1, :]
                for at_, src in ((0, ln_g[l].rearrange("i (c p) -> (i c) p", p=P)),
                                 (24, ln_b[l].rearrange("i (c p) -> (i c) p", p=P)),
                                 (48, out_g_a[l].rearrange("(c p) -> c p", p=P)),
                                 (54, out_g_c[l].rearrange("(c p) -> c p", p=P)),
                                 (56, conv_w[l].rearrange("j (c p) -> (j c) p", p=P)),
                                 (64, conv_b[l].rearrange("(c p) -> c p", p=P)),
                                 (66, lru_br[l].rearrange("(c p) -> c p", p=P)),
                                 (68, lru_bi[l].rearrange("(c p) -> c p", p=P)),
                                 (70, lru_lam[l].rearrange("(c p) -> c p", p=P))):
                    pool.dma_start(r0[at_:at_ + src.shape[0], :], src).then_inc(rows_in, 16)
                gb = out_g_b[l].rearrange("(k g d) -> k g d", k=2, g=4)
                for k in range(2):
                    pool.dma_start(r0[50:54, k * HD:(k + 1) * HD], gb[k]).then_inc(rows_in, 16)
                for c in range(2):
                    pool.dma_start(r1[c * 24:c * 24 + 24, :],
                                   state_c_conv[l].rearrange("b j n -> (b j) n")[:, c * P:(c + 1) * P]).then_inc(rows_in, 16)
                    pool.dma_start(r1[48 + c * 8:56 + c * 8, :], state_c_h[l][:, c * P:(c + 1) * P]).then_inc(rows_in, 16)
            for l in range(DEPTH):
                for n in range(4):
                    for kv, w in enumerate((cmp_wk, cmp_wv)):
                        for h in range(2):
                            o = kv * P + h * HD
                            pool.dma_start(cmp_w[n * CMP:(n + 1) * CMP, l, o:o + HD], w[l]).then_inc(small_in, 16)
                pool.dma_start(gate_bias[:, l, :], b_gate[l].unsqueeze(0).to_broadcast([P, N_GATES])).then_inc(small_in, 16)
            for l in range(DEPTH):
                if l:
                    pool.wait_ge(finals_ready, l)
                else:
                    pool.wait_ge(cleared, 1)
                for n in range(4):
                    a, c = (n % 2) * HD, n // 2
                    for i, w in enumerate((lru_wr, lru_wi)):
                        pool.dma_start(lru_w[a:a + HD, c * 2 + i, a:a + HD], w[l, n]).then_inc(lru_w_in, 16)
                pool.wait_ge(tok_ready, (l + 1) * 12)
                for col, width, out_p, out_s in ((AK, 512, a_prompt, a_sample), (BC, 256, bc_prompt, bc_sample),
                                                 (BS, 256, bs_prompt, bs_sample), (BW, 256, bw_prompt, bw_sample)):
                    if len(out_p.shape) == 7:
                        dst = out_p[l, 0].rearrange("g r a h d -> r g (a h d)")
                    else:
                        dst = out_p[l, 0].rearrange("(t r) a h d -> r t (a h d)", r=P)
                    pool.dma_start(dst, tokens[:, :, col:col + width]).then_inc(rows_stored, 16)
                    pool.dma_start(out_s[l, :, 0].rearrange("b a h d -> b (a h d)"),
                                   samples[:, col:col + width]).then_inc(rows_stored, 16)
                pool.wait_ge(state_ready, l + 1)
                pool.dma_start(h_prompt[l], finals_t[0:1, :]).then_inc(states_stored, 16)
                pool.dma_start(h_sample[l], finals_t[1:9, :]).then_inc(states_stored, 16)
                pool.dma_start(conv_prompt[l, 0], finals_t[9:12, :]).then_inc(states_stored, 16)
                pool.dma_start(conv_sample[l].rearrange("b j n -> (b j) n"), finals_t[12:36, :]).then_inc(states_stored, 16)
            pool.wait_ge(stage_ready, 6)
            pool.dma_start(y_prompt[0].rearrange("(t p) d -> p t d", p=P), stage[:, 0:TT, :]).then_inc(y_stored, 16)
            pool.dma_start(y_sample.rearrange("b s d -> (b s) d"), stage[0:DEC, TT, :]).then_inc(y_stored, 16)
            pool.wait_ge(rows_stored, 16 * 8 * DEPTH)
            pool.wait_ge(states_stored, 16 * 4 * DEPTH)
            pool.wait_ge(y_stored, 32)

        @block.tensor
        def _(pe):
            seen, made = Tally(), Tally()

            def bank_v():
                n = made.next("v tiles")
                if n > 2:
                    pe.wait_ge(v_free, n - 2)
                return banks[(n - 1) % 2]

            def bank_a():
                n = made.next(a_full)
                if n > 2:
                    pe.wait_ge(a_free, n - 2)
                return banks[2 + (n - 1) % 2]

            def bank_s():
                n = made.next(s_full)
                if n > 3:
                    pe.wait_ge(s_free, n - 3)
                return banks[5 + (n - 1) % 3]

            mm = nc.tensor.matmul

            def part(*a, **k):
                return mm(*a, skip_group_check=True, **k)

            pe.wait_ge(consts_in, 16)
            pe.wait_ge(x_in, 32)
            for c in range(KC):
                out = bank_v()
                for t in range(3):
                    r, col, _ = rows_of(t)
                    last = nc.tensor.transpose(out[:, col], stage[0:r, t, c * P:(c + 1) * P], ident[0:r, 0:r])
                last.then_inc(v_full, 1)
            pe.wait_ge(rows_in, 16 * 15 * DEPTH)
            for l in range(DEPTH):
                out = bank_v()
                nc.tensor.transpose(out[:, 0:72], rows[0:72, 2 * l, :], ident[0:72, 0:72])
                nc.tensor.transpose(out[:, 128:192], rows[0:64, 2 * l + 1, :], ident[0:64, 0:64]).then_inc(v_full, 1)

            def wait_x(l, phase):
                pe.wait_ge(x_ready, KC * (1 + 3 * l + phase))

            def ffn(l, j, base):
                f = 2 * l + j
                wait_x(l, 2 * j)
                pe.wait_ge(v_free, made.now("v tiles"))

                def group(k, value, n0):
                    w = slot(k).rearrange("p (w c f) -> p w c f", w=2, c=KC)
                    pe.wait_ge(landed[k % SLOTS], value)
                    for q in range(2):
                        if not isinstance(n0, int) or f or n0 + q >= 2:
                            pe.wait_ge(hidden_done, n0 + (f * FC + q - 1))
                        for i, full in ((0, gate_full), (1, up_full)):
                            for c in range(KC):
                                last = mm(banks[2 * q + i][:, 0:TOK], w[:, i, c, q * P:(q + 1) * P], x[:, c, :],
                                          start=(c == 0), stop=(c == KC - 1))
                            last.then_inc(full, 1)

                for g in range(SLOTS):
                    group(base + g, landed_value(l, base + g), 2 * g)
                with pe.Fori(1, LOOPED) as i:
                    for s in range(SLOTS):
                        group(base + s, landed_value(l, base + s) + i * 32, i * (2 * SLOTS) + 2 * s)
                for g in range(LOOPED * SLOTS, FFN_GROUPS):
                    group(base + g, landed_value(l, base + g), 2 * g)

                def down(g):
                    k = base + FFN_GROUPS + g
                    w = slot(k)[:, 0:FC * P].rearrange("p (c d) -> p c d", c=FC)
                    pe.wait_ge(landed[k % SLOTS], landed_value(l, k))
                    return w

                pe.wait_ge(hidden_done, (f + 1) * FC)
                residual(3 * l + 2 * j, down, lambda w, c, g: w[:, c, :], hidden, FC)

            def residual(n, weights_of, pick, source, chunks):
                def stats(g):
                    pe.wait_ge(sq_done, n * KC + g + 1)
                    mm(banks[6][:, 0:TOK], mean_w, z[:, g, :], start=(g == 0), stop=(g == KC - 1), skip_group_check=True)
                    mm(banks[7][:, 0:TOK], mean_w, squares_ffn(g), start=(g == 0), stop=(g == KC - 1),
                       skip_group_check=True).then_inc(stat_done, 1)

                for g in range(KC):
                    w = weights_of(g)
                    if g >= 2:
                        pe.wait_ge(z_done, n * KC + g - 1)
                    for c in range(chunks):
                        last = mm(banks[4 + g % 2][:, 0:TOK], pick(w, c, g), source[:, c, :],
                                  start=(c == 0), stop=(c == chunks - 1))
                    last.then_inc(y_full, 1)
                    if g:
                        stats(g - 1)
                stats(KC - 1)

            def mix(l):
                wait_x(l, 1)
                for g in range(4):
                    k = WIN_USE + g
                    w = slot(k).rearrange("p (c n) -> p c n", c=KC)
                    pe.wait_ge(landed[k % SLOTS], landed_value(l, k))
                    for t in range(3):
                        r, col, _ = rows_of(t)
                        out = bank_v()
                        for c in range(KC):
                            last = mm(out[0:r, :], x[:, c, col], w[:, c, :], start=(c == 0), stop=(c == KC - 1))
                        last.then_inc(v_full, 1)
                pe.wait_ge(gate_w_in, 16 * (l + 1))
                for t in range(3):
                    r, col, _ = rows_of(t)
                    out = bank_v()
                    for c in range(KC):
                        last = mm(out[0:r, 0:N_GATES], x[:, c, col], gate_w[:, c, :], start=(c == 0), stop=(c == KC - 1))
                    last.then_inc(v_full, 1)
                k = WIN_USE + 4
                w = slot(k).rearrange("p (c n) -> p c n", c=KC)
                pe.wait_ge(landed[k % SLOTS], landed_value(l, k))
                for m in range(4):
                    out = bank_v() if m < 2 else bank_a()
                    for c in range(KC):
                        last = mm(out[:, 0:TOK], w[:, c, m * P:(m + 1) * P], x[:, c, :], start=(c == 0), stop=(c == KC - 1))
                    last.then_inc(v_full if m < 2 else a_full, 1)
                pe.wait_ge(tok_ready, 12 * (l + 1))
                for n, col_t in enumerate((AQ, AQ + P, AK, AK + P, BQ, BQ + P, BQ + 2 * P, BQ + 3 * P, BS, BW)):
                    out = bank_a()
                    for t in range(3):
                        r, col, src = rows_of(t)
                        last = nc.tensor.transpose(out[:, col], src[:, col_t:col_t + P], ident[0:r, 0:r])
                    last.then_inc(a_full, 1)
                feats_tiles[0] = made.now(a_full)
                pe.wait_ge(lru_w_in, 16 * 8 * (l + 1))
                pe.wait_ge(xc_ready, l + 1)
                for c in range(2):
                    for i in range(2):
                        out = bank_a()
                        mm(out[:, 0:TOK], lru_w[:, c * 2 + i, :], xc[:, c, :], start=True, stop=True).then_inc(a_full, 1)
                pe.wait_ge(finals_ready, l + 1)
                out = bank_v()
                nc.tensor.transpose(out[0:36, 0:P], finals[:, 0, :], ident)
                nc.tensor.transpose(out[0:36, P:2 * P], finals[:, 1, :], ident).then_inc(v_full, 1)
                prompt(l)
                for hf in range(2):
                    sample(l, hf)
                for c in range(KC):
                    pe.wait_ge(rms_sq, l * KC + c + 1)
                    g = 0 if c < 2 else 1 if c < 6 else 2
                    mm(banks[4 + g][:, 0:TOK], mean_w, squares[:, c % 2, :], start=c in (0, 2, 6), stop=c in (1, 5, 7))\
                        .then_inc(rms_stat, 1)
                pe.wait_ge(yn_ready, KC * (l + 1))

                def weights_of(g):
                    k = WOUT_USE + g // 4
                    if g % 4 == 0:
                        pe.wait_ge(landed[k % SLOTS], landed_value(l, k))
                    return slot(k).rearrange("p (c n) -> p c n", c=KC)

                residual(3 * l + 1, weights_of, lambda w, c, g: w[:, c, (g % 4) * P:(g % 4 + 1) * P], mixed, KC)

            feats_tiles = [0]

            def prompt(l):
                pe.wait_ge(a_free, feats_tiles[0])
                pe.wait_ge(prod_ready, l + 1)
                out = bank_v()
                for t in range(TT):
                    part(out[:, 4 * t:4 * t + 4], prod_c[:, t, 0:P], table_of("sel4"), start=(t == 0), stop=False)
                rep = table_of("selrep").rearrange("p (t n) -> p t n", t=TT)
                for t in range(TT):
                    last = part(out[0:HD, P:2 * P], rep[:, t, :], prod_c[:, t, P:2 * P], start=False, stop=(t == 1))
                last.then_inc(v_full, 1)
                pe.wait_ge(cmp_ready, l + 1)
                for qb in range(TT):
                    q_cols = slice(qb * P, (qb + 1) * P)
                    nk = (qb + 1) * P
                    done = l * 2 * 10 + qb * 10

                    def scores(u):
                        out = bank_s()[:, :].rearrange("p (b n) -> p b n", b=2)
                        for i in range(2):
                            if u < 2:
                                a, q, key = u * HD, i, 2 + i
                            else:
                                a, q, key = ((u - 2) % 2) * HD, 4 + (u - 2) // 2, 8 + i
                            last = part(out[:, i, 0:nk], feats[a:a + HD, q, q_cols], feats[a:a + HD, key, 0:nk],
                                        start=(i == 0), stop=(i == 1))
                        last.then_inc(s_full, 1)

                    def turn(u):
                        pe.wait_ge(probs_ready, done + u + 1 + (2 * l + qb + 1))
                        out = bank_a()
                        for i in range(2):
                            for kt in range(qb + 1):
                                n = i * (qb + 1) + kt
                                last = nc.tensor.transpose(out[:, n * P:(n + 1) * P],
                                                           probs[:, (done + u) % 3, i, kt * P:(kt + 1) * P], ident)
                        last.then_inc(a_full, 1)
                        turned[u] = made.now(a_full)

                    turned = {}
                    opened = [None]

                    def values(u):
                        pe.wait_ge(a_free, turned[u])
                        pt = probs_t[:, (done + u) % 2, :]
                        if u < 2:
                            if u == 0:
                                opened[0] = bank_v()
                            out = opened[0]
                            for i in range(2):
                                for kt in range(qb + 1):
                                    n = i * (qb + 1) + kt
                                    v = AV + (2 * i + u) * HD
                                    last = part(out[u * HD:(u + 1) * HD, i * P:(i + 1) * P], tokens[:, kt, v:v + HD],
                                                pt[:, n * P:(n + 1) * P], start=(i == 0 and kt == 0), stop=(kt == qb))
                            last.then_inc(pv_done, 1)
                            return
                        g, kv = (u - 2) // 2, (u - 2) % 2
                        if kv == 0:
                            opened[0] = bank_v()
                            part(opened[0][:, 0:P], vcmp[0:HD, g * P:(g + 1) * P], pc_t[0:HD, :], start=True, stop=False)
                        out = opened[0]
                        for i, base in enumerate((BS, BW)):
                            for kt in range(qb + 1):
                                n = i * (qb + 1) + kt
                                v = base + P + kv * HD
                                last = part(out[kv * HD:(kv + 1) * HD, 0:P], tokens[:, kt, v:v + HD],
                                            pt[:, n * P:(n + 1) * P], start=False, stop=(i == 1 and kt == qb))
                        last.then_inc(pv_done, 1)

                    for k in range(2):
                        out = bank_s()
                        for g in range(4):
                            last = part(out[:, g * 8:g * 8 + 8], feats[k * HD:(k + 1) * HD, 4 + g, q_cols],
                                        kcmp[k * HD:(k + 1) * HD, :], start=(g == 0), stop=(g == 3))
                        last.then_inc(s_full, 1)
                    scores(0)
                    scores(1)
                    pe.wait_ge(probs_ready, done + 1 + (2 * l + qb))
                    out = bank_a()
                    nc.tensor.transpose(out[0:HD, 0:P], pc[:, :], ident).then_inc(a_full, 1)
                    for u in range(10):
                        turn(u)
                        if u + 2 < 10:
                            scores(u + 2)
                        if u:
                            values(u - 1)
                    values(9)

            def sample(l, hf):
                n = 2 * l + hf
                for b in range(HALF):
                    for half in range(2):
                        m = (n * HALF + b) * 2 + half
                        pe.wait_ge(bc_weighted, m + 1)
                        for i in range(4):
                            page = half * 4 + i
                            prod = bc_pages[:, m % 2, i, :]
                            mm(banks[5][:, b * CMP + page * 4:b * CMP + page * 4 + 4], prod[:, 0:P], table_of("sel4"),
                               start=True, stop=True)
                            last = part(banks[6][0:CMP, b * P:(b + 1) * P],
                                        table_of("selw")[:, 28 - 4 * page:60 - 4 * page], prod[:, P:2 * P],
                                        start=(page == 0), stop=(page == 7))
                        last.then_inc(bc_used, 1)
                pe.wait_ge(cmp_out, n + 1)
                pe.wait_ge(q_ready, n + 1)
                pe.wait_ge(gates_ready, 3 * (l + 1))
                misc = banks[4]
                b0 = SEQ + hf * HALF

                def qb_(b):
                    return q_b[:, b * RB:(b + 1) * RB]

                def qa_(b, c):
                    return q_a[:, (b * 2 + c) * RA:(b * 2 + c + 1) * RA]

                for b in range(HALF):
                    part(misc[0:RB, 256:288], qb_(b), kcmp_s[:, b * CMP:(b + 1) * CMP], start=(b == 0), stop=False)
                for b in range(HALF):
                    for i in range(2):
                        part(misc[0:RB, 288 + i:289 + i], qb_(b), feats[:, 8 + i, b0 + b:b0 + b + 1], start=False, stop=False)
                    for c in range(2):
                        part(misc[0:RA, 290:291], qa_(b, c), feats[:, 2 + c, b0 + b:b0 + b + 1], start=False, stop=False)
                pending = []

                def multiply(b, i, m, tile):
                    pe.wait_ge(a_free if i % 2 else v_free, tile)
                    kt = key_t[:, m % 4, :]
                    if i < 3:
                        last = part(banks[5 + i][0:RB, :], qb_(b), kt, start=(b == 0), stop=(b == HALF - 1))
                    else:
                        for c in range(2):
                            last = part(misc[0:RA, 0:256], qa_(b, c), kt[:, c * 256:(c + 1) * 256],
                                        start=False, stop=(b == HALF - 1 and c == 1))
                    last.then_inc(kt_used, 1)

                for b in range(HALF):
                    s = b
                    pe.wait_ge(ring_in[s], 16 * 12 * (n + 1))
                    for i in range(4):
                        m = (n * HALF + b) * 4 + i
                        out = bank_a() if i % 2 else bank_v()
                        for j in range(4):
                            if i < 3:
                                src = ring[:, s, (4 * i + j) * 256:(4 * i + j) * 256 + P]
                            else:
                                c, kt = j // 2, j % 2
                                src = ring[:, s, 3072 + kt * 512 + c * P:3072 + kt * 512 + (c + 1) * P]
                            last = nc.tensor.transpose(out[:, j * P:(j + 1) * P], src, ident)
                        last.then_inc(a_full if i % 2 else v_full, 1)
                        pending.append((b, i, m, made.now(a_full if i % 2 else "v tiles")))
                        if len(pending) > 2:
                            multiply(*pending.pop(0))
                while pending:
                    multiply(*pending.pop(0))
                out = bank_v()
                ex = table_of("expand", DEC).rearrange("p (h r) -> p h r", h=2)
                mm(out[0:RB, 0:N_GATES], ex[:, hf, :], gates[0:DEC, 2, :], start=True, stop=True).then_inc(v_full, 1)
                pe.wait_ge(imp_ready, n + 1)
                out = bank_v()
                mm(out[0:RB, 0:CMP], table_of("same", RB), s_cmp[0:RB, :], start=True, stop=True).then_inc(v_full, 1)
                pe.wait_ge(s_probs, n + 1)
                out = bank_v()
                idb, ida = ident[0:RB, 0:RB], ident[0:RA, 0:RA]
                for t in range(12):
                    src = s_sel[0:RB, t * P:(t + 1) * P] if t < 8 else s_win[0:RB, (t - 8) * P:(t - 7) * P]
                    nc.tensor.transpose(out[:, t * RB:(t + 1) * RB], src, idb)
                nc.tensor.transpose(out[0:CMP, 384:416], s_cmp[0:RB, :], idb)
                nc.tensor.transpose(out[0:DEC, 416:448], own_p[0:RB, 0:8], idb)
                nc.tensor.transpose(out[0:DEC, 448:480], own_p[0:RB, 8:16], idb).then_inc(v_full, 1)
                out = bank_v()
                for t in range(2):
                    nc.tensor.transpose(out[:, t * RA:(t + 1) * RA], s_a[0:RA, t * P:(t + 1) * P], ida)
                nc.tensor.transpose(out[0:DEC, 2 * RA:3 * RA], own_p[0:RA, 16:24], ida).then_inc(v_full, 1)
                pe.wait_ge(s_pt, n + 1)
                out = bank_v()
                part(out[:, 0:RB], samples[:, BS + P:BS + 2 * P], p_t[0:DEC, 416:448], start=True, stop=False)
                part(out[:, 0:RB], samples[:, BW + P:BW + 2 * P], p_t[0:DEC, 448:480], start=False, stop=False)
                for c in range(2):
                    part(out[:, RB + c * RA:RB + (c + 1) * RA], samples[:, AV + c * P:AV + (c + 1) * P],
                         p_t[0:DEC, 480 + 2 * RA:480 + 3 * RA], start=False, stop=False)
                for b in range(HALF):
                    cols = slice(b * 8, b * 8 + 8)
                    for t in range(12):
                        part(out[:, cols], ring[:, b, t * 256 + P:(t + 1) * 256],
                             p_t[:, t * RB + b * 8:t * RB + b * 8 + 8], start=False, stop=False)
                    part(out[:, cols], vcmp_s[0:CMP, b * P:(b + 1) * P], p_t[0:CMP, 384 + b * 8:392 + b * 8],
                         start=False, stop=True)
                    for c in range(2):
                        o = RB + c * RA + b * 4 + 2 * c
                        for kt in range(2):
                            last = part(out[:, o:o + 2], ring[:, b, 3328 + kt * 512 + c * P:3328 + kt * 512 + (c + 1) * P],
                                        p_t[:, 480 + kt * RA + b * 4 + 2 * c:480 + kt * RA + b * 4 + 2 * c + 2],
                                        start=False, stop=(kt == 1))
                    last.then_inc(ring_used, 1)

            def squares_ffn(g):
                return squares[:, g % 2, :]

            for l in range(DEPTH):
                ffn(l, 0, 0)
                mix(l)
                ffn(l, 1, WOUT_USE + 2)
            wait_x(DEPTH, 0)
            for t in range(3):
                r, col, _ = rows_of(t)
                for half in range(2):
                    out = bank_v()
                    for c in range(4):
                        last = nc.tensor.transpose(out[0:r, c * P:(c + 1) * P], x[:, half * 4 + c, col], ident)
                    last.then_inc(v_full, 1)

        @block.scalar
        def _(act):
            made = Tally()
            go = nc.scalar.activation

            def bank_a():
                n = made.next(a_full)
                act.wait_ge(a_full, n)
                return banks[2 + (n - 1) % 2]

            def own():
                act.wait_ge(act_own, made.now(act_own))

            def mark(ins):
                made.next(act_own)
                return ins.then_inc(act_own, 1)

            act.wait_ge(var_done, 1)
            go(rstd[:, 0, 0:4], rstd[:, 0, 0:4], ACT.Exp).then_inc(std_done, 1)

            def square_chunks(n):
                for g in range(KC):
                    act.wait_ge(z_done, n * KC + g + 1)
                    if n * KC + g >= 2:
                        act.wait_ge(stat_done, n * KC + g - 1)
                    go(squares[:, g % 2, :], z[:, g, :], ACT.Square).then_inc(sq_done, 1)
                norm(n)

            def norm(n):
                l, i = n // 3, n % 3
                act.wait_ge(var_done, n + 2)
                go(rstd[:, 0, :], rstd[:, 0, :], ACT.Sqrt).then_inc(std_done, 1)
                for c in range(KC):
                    act.wait_ge(norm_done, n * KC + c + 1)
                    go(x[:, c, :], z[:, c, :], ACT.Identity, bias=params[:, l, 24 + i * 8 + c:25 + i * 8 + c],
                       scale=params[:, l, i * 8 + c:i * 8 + c + 1]).then_inc(x_ready, 1)

            def ffn(l, j):
                f = 2 * l + j

                def chunk(n, q, always):
                    act.wait_ge(gate_full, n + (f * FC + q + 1))
                    if always:
                        act.wait_ge(hidden_done, n + (f * FC + q - 1))
                    go(silu[:, q, :], banks[2 * q][:, 0:TOK], ACT.Silu).then_inc(silu_done, 1)

                for q in range(2):
                    chunk(0, q, f > 0)
                with act.Fori(1, FC // 2) as i:
                    for q in range(2):
                        chunk(i * 2, q, True)
                square_chunks(3 * l + 2 * j)

            def mix(l):
                act.wait_ge(gates_raw, l + 1)
                for t in range(3):
                    r, _, _ = rows_of(t)
                    go(gates[0:r, t, :], gates[0:r, t, :], ACT.Sigmoid).then_inc(gates_ready, 1)
                for c in range(2):
                    ps = bank_a()
                    go(gelu[:, c, :], ps[:, 0:TOK], ACT.Gelu_apprx_tanh).then_inc(a_free, 1)
                for n in range(10):
                    ps = bank_a()
                    go(feats[:, n, :], ps[:, 0:TOK], ACT.Copy).then_inc(a_free, 1)
                for c in range(2):
                    for i, dst in enumerate((lru_r, lru_i)):
                        ps = bank_a()
                        go(dst[:, c, :], ps[:, 0:TOK], ACT.Sigmoid,
                           bias=params[:, l, 66 + 2 * i + c:67 + 2 * i + c]).then_inc(a_free, 1)
                act.wait_ge(a_free, made.now(a_full))
                for c in range(2):
                    go(lru_t[:, c, :], lru_r[:, c, :], ACT.Tanh, scale=decay[:, l, c:c + 1]).then_inc(gate_r, 1)
                for c in range(2):
                    go(rstd[:, c, :], lru_r[:, c, :], ACT.Exp, scale=decay[:, l, c:c + 1]).then_inc(gate_r, 1)
                act.wait_ge(lru_f, l + 1)
                for c in range(2):
                    go(lru_t[:, c, :], lru_t[:, c, :], ACT.Sqrt, scale=-1.0).then_inc(lru_s, 1)
                for qb in range(TT):
                    nk = (qb + 1) * P
                    done = (2 * l + qb) * 10
                    act.wait_ge(masked, done + (2 * l + qb) + 1)
                    go(pc[:, :], pc[:, :], ACT.Exp).then_inc(exps, 1)

                    def exp_unit(u):
                        act.wait_ge(masked, done + (2 * l + qb) + 2 + u)
                        r = (done + u) % 3
                        for i in range(2):
                            last = go(probs[:, r, i, 0:nk], probs[:, r, i, 0:nk], ACT.Exp,
                                      bias=stat[:, (done + u) % 4, i:i + 1],
                                      accum_out=stat[:, (done + u) % 4, 2 + i:3 + i])
                        last.then_inc(exps, 1)

                    def evac(u):
                        if done + u >= 2:
                            act.wait_ge(pv_done, done + u - 1)
                        ps = bank_a()
                        n = 2 * (qb + 1) * P
                        go(probs_t[:, (done + u) % 2, 0:n], ps[:, 0:n], ACT.Copy).then_inc(a_free, 1)

                    exp_unit(0)
                    if qb or l:
                        act.wait_ge(pv_done, done)
                    ps = bank_a()
                    go(pc_t[0:HD, :], ps[0:HD, 0:P], ACT.Copy).then_inc(a_free, 1)
                    for u in range(1, 10):
                        exp_unit(u)
                        evac(u - 1)
                    evac(9)
                for hf in range(2):
                    n = 2 * l + hf
                    for b in range(HALF):
                        for i in (1, 3):
                            m = (n * HALF + b) * 4 + i
                            if m >= 4:
                                act.wait_ge(kt_used, m - 3)
                            ps = bank_a()
                            go(key_t[:, m % 4, :], ps[:, :], ACT.Copy).then_inc(a_free, 1)
                    act.wait_ge(s_masked, 4 * n + 1)
                    go(s_cmp[0:RB, :], s_cmp[0:RB, :], ACT.Exp, bias=s_stat[0:RB, 0:1], accum_out=s_stat[0:RB, 8:9])\
                        .then_inc(s_exps, 1)
                    act.wait_ge(s_masked, 4 * n + 2)
                    go(s_win[0:RB, :], s_win[0:RB, :], ACT.Exp, bias=s_stat[0:RB, 1:2], accum_out=s_stat[0:RB, 9:10])\
                        .then_inc(s_exps, 1)
                    act.wait_ge(s_masked, 4 * n + 3)
                    go(s_a[0:RA, :], s_a[0:RA, :], ACT.Exp, bias=s_stat[0:RA, 2:3], accum_out=s_stat[0:RA, 10:11])\
                        .then_inc(s_exps, 1)
                    act.wait_ge(s_masked, 4 * n + 4)
                    go(s_sel[0:RB, :], s_sel[0:RB, :], ACT.Exp, bias=s_stat[0:RB, 3:4], accum_out=s_stat[0:RB, 11:12])\
                        .then_inc(s_exps, 1)
                act.wait_ge(mix_ready, l + 1)
                for c in range(KC):
                    if c >= 2:
                        act.wait_ge(rms_stat, l * KC + c - 1)
                    go(squares[:, c % 2, :], mixed[:, c, :], ACT.Square).then_inc(rms_sq, 1)
                act.wait_ge(rms_stat, (l + 1) * KC)
                for g, widths in enumerate((4.0, 2.0, 4.0)):
                    go(rstd[:, g, :], banks[4 + g][:, 0:TOK], ACT.Sqrt, bias=eps[:, 1:2], scale=widths).then_inc(rms_std, 1)
                square_chunks(3 * l + 1)

            for l in range(DEPTH):
                ffn(l, 0)
                mix(l)
                ffn(l, 1)

        @block.vector
        def _(dve):
            made = Tally()
            tt, ts, stt, copy = nc.vector.tensor_tensor, nc.vector.tensor_scalar, nc.vector.scalar_tensor_tensor, nc.vector.tensor_copy
            reduce = nc.vector.tensor_reduce

            def bank_v(full=v_full, value=None):
                n = made.next("v tiles")
                dve.wait_ge(full, made.next(v_full) if value is None else value)
                return banks[(n - 1) % 2]

            def free_v(ins):
                ins.then_inc(v_free, 1)

            def v_read():
                dve.wait_ge(v_free, made.now("v tiles"))

            def step(ins):
                ins.then_inc(vec, 1)
                dve.wait_ge(vec, made.next(vec))

            def mark(ins):
                ins.then_inc(vec, 1)
                made.next(vec)

            def settle():
                dve.wait_ge(vec, made.now(vec))

            mark(nc.vector.memset(eps[:, 0:1], EPS / ALPHA ** 2))
            mark(nc.vector.memset(eps[:, 1:2], EPS))
            for c in range(KC):
                ps = bank_v()
                free_v(copy(x[:, c, :], ps[:, 0:TOK]))
            v_read()
            dve.sem_inc(x_ready, KC)
            for l in range(DEPTH):
                ps = bank_v()
                copy(params[:, l, :], ps[:, 0:72])
                free_v(copy(states[:, l, :], ps[:, 128:192]))
            v_read()
            lam = params[:, :, 70:72]
            e = rstd[:, 0, 0:4].rearrange("p (l c) -> p l c", l=2)
            s1, s2, s3 = (rstd[:, 1, 4 * i:4 * i + 4].rearrange("p (l c) -> p l c", l=2) for i in range(3))
            step(ts(s1, lam, -1.0, None, ALU.mult))
            tt(e, lam, s1, ALU.min).then_inc(var_done, 1)
            dve.wait_ge(std_done, 1)
            step(ts(s2, e, 2.0, None, ALU.add))
            step(nc.vector.reciprocal(s2, s2))
            step(tt(e, e, s2, ALU.mult))
            step(tt(s2, e, e, ALU.mult))
            step(ts(s3, s2, 1.0 / 15, 1.0 / 13, ALU.mult, ALU.add))
            for odd in (11, 9, 7, 5, 3, 1):
                step(tt(s3, s3, s2, ALU.mult))
                step(ts(s3, s3, 1.0 / odd, None, ALU.add))
            step(tt(s3, s3, e, ALU.mult))
            step(ts(s1, s1, 0.0, None, ALU.max))
            step(stt(s3, s3, 2.0, s1, ALU.mult, ALU.add))
            step(ts(decay[:, :, :], s3, -LRU_C, None, ALU.mult))

            def residual(n, factor):
                for g in range(KC):
                    dve.wait_ge(y_full, n * KC + g + 1)
                    stt(z[:, g, :], banks[4 + g % 2][:, 0:TOK], factor, x[:, g, :], ALU.mult, ALU.add).then_inc(z_done, 1)
                dve.wait_ge(stat_done, (n + 1) * KC)
                step(copy(mean_sb[:, :], banks[6][:, 0:TOK]))
                v = rstd[:, 0, :]
                step(stt(v, mean_sb[:, :], -1.0, mean_sb[:, :], ALU.mult, ALU.mult))
                step(tt(v, banks[7][:, 0:TOK], v, ALU.add))
                ts(v, v, 0.0, eps[:, 0:1], ALU.max, ALU.add).then_inc(var_done, 1)
                dve.wait_ge(std_done, n + 2)
                step(nc.vector.reciprocal(v, v))
                mark(tt(z[:, 0, :], z[:, 0, :], mean_sb[:, :], ALU.subtract))
                for c in range(KC):
                    settle()
                    if c + 1 < KC:
                        mark(tt(z[:, c + 1, :], z[:, c + 1, :], mean_sb[:, :], ALU.subtract))
                    tt(z[:, c, :], z[:, c, :], v, ALU.mult).then_inc(norm_done, 1)

            def ffn(l, j):
                f = 2 * l + j

                def chunk(n, q, out):
                    dve.wait_ge(silu_done, n + (f * FC + q + 1))
                    dve.wait_ge(up_full, n + (f * FC + q + 1))
                    tt(out, silu[:, q, :], banks[2 * q + 1][:, 0:TOK], ALU.mult).then_inc(hidden_done, 1)

                if f:
                    dve.wait_ge(rows_stored, 16 * 8 * (l + j))
                    dve.wait_ge(states_stored, 16 * 4 * (l + j))
                with dve.Fori(0, FC // 2) as i:
                    for q in range(2):
                        chunk(i * 2, q, hidden[:, bass.ds(i * 2 + q, 1), :].rearrange("p c t -> p (c t)"))
                residual(3 * l + 2 * j, 0.5 / ALPHA)

            def rope(ps, col, heads, dst, t, r):
                cos = table_of("cos", r)[:, t * HD:(t + 1) * HD].unsqueeze(1)
                sin = table_of("sin", r)[:, t * HD:(t + 1) * HD].unsqueeze(1)
                src = ps[0:r, col:col + heads * HD].rearrange("p (h d) -> p h d", h=heads)
                t1 = rope_t[0:r, 0, 0:heads * HD].rearrange("p (h d) -> p h d", h=heads)
                t2 = rope_t[0:r, 1, 0:heads * HD].rearrange("p (h d) -> p h d", h=heads)
                hf = HD // 2
                tt(t1, src, cos.to_broadcast([r, heads, HD]), ALU.mult)
                tt(t2[:, :, 0:hf], src[:, :, hf:HD], sin[:, :, 0:hf].to_broadcast([r, heads, hf]), ALU.mult)
                step(tt(t2[:, :, hf:HD], src[:, :, 0:hf], sin[:, :, hf:HD].to_broadcast([r, heads, hf]), ALU.mult))
                return tt(dst, t1, t2, ALU.add)

            def mix(l):
                par = params[:, l, :]
                if l == 0:
                    dve.wait_ge(small_in, 16 * 17 * DEPTH)
                for g in range(4):
                    for t in range(3):
                        r, _, tok = rows_of(t)
                        ps = bank_v()
                        heads = lambda a, n: tok[:, a:a + n * HD].rearrange("p (h d) -> p h d", h=n)
                        bq = tok[:, BQ:BQ + 512].rearrange("p (g k d) -> p g k d", g=4, k=2)
                        if g == 0:
                            last = rope(ps, 0, 8, heads(AQ, 8), t, r)
                        elif g == 1:
                            rope(ps, 256, 4, bq[:, :, 0, :], t, r)
                            last = copy(tok[:, AV:AV + 256], ps[0:r, 0:256])
                        elif g == 2:
                            mark(rope(ps, 0, 4, bq[:, :, 1, :], t, r))
                            settle()
                            rope(ps, 256, 2, heads(BC, 2), t, r)
                            last = copy(tok[:, BC + P:BC + 2 * P], ps[0:r, 384:512])
                        else:
                            mark(rope(ps, 0, 2, heads(BS, 2), t, r))
                            settle()
                            rope(ps, 256, 2, heads(BW, 2), t, r)
                            copy(tok[:, BS + P:BS + 2 * P], ps[0:r, P:2 * P])
                            last = copy(tok[:, BW + P:BW + 2 * P], ps[0:r, 384:512])
                        free_v(last)
                        v_read()
                        dve.sem_inc(tok_ready, 1)
                for t in range(3):
                    r, _, _ = rows_of(t)
                    ps = bank_v()
                    free_v(tt(gates[0:r, t, :], ps[0:r, 0:N_GATES], gate_bias[0:r, l, :], ALU.add))
                v_read()
                dve.sem_inc(gates_raw, 1)
                mark(nc.vector.memset(conv_x[:, :, 0:3], 0.0))
                for c in range(2):
                    ps = bank_v()
                    copy(conv_x[:, c, 3:259], ps[:, 0:SEQ])
                    copy(conv_s[:, c, :, 0:3], states[:, l, c * 24:c * 24 + 24].rearrange("p (b j) -> p b j", b=DEC))
                    free_v(copy(conv_s[:, c, :, 3], ps[:, SEQ:TOK]))
                v_read()
                for c in range(2):
                    for j in range(4):
                        wj = par[:, 56 + 2 * j + c:57 + 2 * j + c]
                        for dst, src in ((xc[:, c, 0:SEQ], conv_x[:, c, j:j + SEQ]), (xc[:, c, SEQ:TOK], conv_s[:, c, :, j])):
                            if j == 0:
                                mark(ts(dst, src, wj, par[:, 64 + c:65 + c], ALU.mult, ALU.add))
                            else:
                                mark(stt(dst, src, wj, dst, ALU.mult, ALU.add))
                        settle()
                dve.sem_inc(xc_ready, 1)
                dve.wait_ge(gate_r, 4 * (l + 1))
                a, th = rstd[:, 0:2, :], lru_t
                ix = xc
                mark(tt(lru_r[:, :, :], a, a, ALU.mult))
                step(tt(ix[:, :, :], lru_i[:, :, :], xc[:, :, :], ALU.mult))
                step(stt(th, lru_r[:, :, :], 1.0, th, ALU.add, ALU.mult))
                dve.sem_inc(lru_f, 1)
                dve.wait_ge(lru_s, 2 * (l + 1))
                step(tt(ix, th, ix, ALU.mult))
                hs = lru_r
                for c in range(2):
                    mark(nc.vector.tensor_tensor_scan(hs[:, c, 0:SEQ], a[:, c, 0:SEQ], ix[:, c, 0:SEQ], 0.0, ALU.mult, ALU.add))
                h0 = states[:, l, 48:64].rearrange("p (c b) -> p c b", c=2)
                step(tt(hs[:, :, SEQ:TOK], a[:, :, SEQ:TOK], h0, ALU.mult))
                step(tt(hs[:, :, SEQ:TOK], hs[:, :, SEQ:TOK], ix[:, :, SEQ:TOK], ALU.add))
                for c in range(2):
                    copy(finals[:, c, 0:1], hs[:, c, SEQ - 1:SEQ])
                    copy(finals[:, c, 1:9], hs[:, c, SEQ:TOK])
                    copy(finals[:, c, 9:12], conv_x[:, c, SEQ:SEQ + 3])
                    mark(copy(finals[:, c, 12:36].rearrange("p (b j) -> p b j", b=DEC), conv_s[:, c, :, 1:4]))
                settle()
                dve.sem_inc(finals_ready, 1)
                mark(tt(mixed[:, 6:8, :], hs, gelu, ALU.mult))
                ps = bank_v()
                free_v(copy(finals_t[0:36, :], ps[0:36, 0:256]))
                v_read()
                dve.sem_inc(state_ready, 1)
                prompt(l)
                for hf in range(2):
                    sample(l, hf)
                v_read()
                dve.sem_inc(mix_ready, 1)
                for g in range(3):
                    dve.wait_ge(rms_std, 3 * l + g + 1)
                    mark(nc.vector.reciprocal(rstd[:, g, :], rstd[:, g, :]))
                settle()
                for c in range(KC):
                    g = 0 if c < 2 else 1 if c < 6 else 2
                    stt(mixed[:, c, :], mixed[:, c, :], par[:, 48 + c:49 + c], rstd[:, g, :], ALU.mult, ALU.mult)\
                        .then_inc(yn_ready, 1)
                residual(3 * l + 1, 1.0 / ALPHA)

            def prompt(l):
                settle()
                for t in range(TT):
                    mark(tt(prod_c[:, t, 0:256], tokens[:, t, BC:BC + 256], cmp_w[:, l, :], ALU.mult))
                settle()
                dve.sem_inc(prod_ready, 1)
                ps = bank_v()
                copy(kcmp[:, :], ps[:, 0:8])
                free_v(tt(vcmp[0:HD, :].rearrange("p (g n) -> p g n", g=4),
                          ps[0:HD, P:2 * P].unsqueeze(1).to_broadcast([HD, 4, P]),
                          table_of("maskv", HD).rearrange("p (g n) -> p g n", g=4), ALU.mult))
                v_read()
                dve.sem_inc(cmp_ready, 1)
                dve.wait_ge(gates_ready, 3 * (l + 1))
                n_s = [(2 * l) * 12]

                def bank_s():
                    n_s[0] += 1
                    dve.wait_ge(s_full, n_s[0])
                    return banks[5 + (n_s[0] - 1) % 3]

                for qb in range(TT):
                    nk = (qb + 1) * P
                    done = (2 * l + qb) * 10
                    p3 = pc[:, :].rearrange("p (h n) -> p h n", h=8)
                    vis_add = table_of("vis_add")[:, qb * 8:qb * 8 + 8].unsqueeze(1).to_broadcast([P, 8, 8])
                    vis = table_of("vis")[:, qb * 8:qb * 8 + 8].unsqueeze(1).to_broadcast([P, 8, 8])
                    for k in range(2):
                        ps = bank_s()
                        stt(pc[:, :].rearrange("p (g k n) -> p g k n", g=4, k=2)[:, :, k, :],
                            ps[:, 0:32].rearrange("p (g n) -> p g n", g=4), SCALE, vis_add[:, 0:4, :],
                            ALU.mult, ALU.add).then_inc(s_free, 1)
                    dve.wait_ge(s_free, n_s[0])
                    mx, sm, gt = pc_stat[:, 0:8], pc_stat[:, 8:16], pc_stat[:, 16:24]
                    step(reduce(mx, p3, AX_X, ALU.max))
                    tt(p3, p3, mx.unsqueeze(2).to_broadcast([P, 8, 8]), ALU.subtract).then_inc(masked, 1)

                    def mask_unit(u):
                        ps = bank_s()[:, :].rearrange("p (b n) -> p b n", b=2)[:, :, 0:nk]
                        m = table_of("mask_a" if u < 2 else "mask_c")[:, qb * SEQ:qb * SEQ + nk].unsqueeze(1)
                        r = (done + u) % 3
                        pr = probs[:, r, :, 0:nk]
                        stt(pr, ps, SCALE, m.to_broadcast([P, 2, nk]), ALU.mult, ALU.add).then_inc(s_free, 1)
                        dve.wait_ge(s_free, n_s[0])
                        reduce(stat[:, (done + u) % 4, 0:2], pr, AX_X, ALU.max, negate=True).then_inc(masked, 1)

                    def norm_unit(u):
                        dve.wait_ge(exps, done + (2 * l + qb) + 2 + u)
                        st = stat[:, (done + u) % 4, :]
                        step(nc.vector.reciprocal(st[:, 4:6], st[:, 2:4]))
                        if u >= 2:
                            h = ((u - 2) % 2) * 4 + (u - 2) // 2
                            step(tt(st[:, 4:6], st[:, 4:6], gates[:, qb, 3 * h + 1:3 * h + 3], ALU.mult))
                        pr = probs[:, (done + u) % 3, :, 0:nk]
                        tt(pr, pr, st[:, 4:6].unsqueeze(2).to_broadcast([P, 2, nk]), ALU.mult).then_inc(probs_ready, 1)

                    def collect(u):
                        if u < 0 or u % 2 == 0:
                            return
                        c = 2 + (u - 2) // 2
                        ps = bank_v(pv_done, done + u + 1)
                        if u == 1:
                            free_v(copy(mixed[:, 0:2, qb * P:(qb + 1) * P], ps[:, 0:2 * P].rearrange("p (c q) -> p c q", c=2)))
                            return
                        free_v(copy(mixed[:, c, qb * P:(qb + 1) * P], ps[:, 0:P]))

                    mask_unit(0)
                    dve.wait_ge(exps, done + (2 * l + qb) + 1)
                    step(tt(p3, p3, vis, ALU.mult))
                    step(reduce(sm, p3, AX_X, ALU.add))
                    step(ts(sm, sm, 1e-30, None, ALU.max))
                    step(nc.vector.reciprocal(sm, sm))
                    gate0 = gates[:, qb, :].rearrange("p (k g t) -> p g k t", k=2, g=4)[:, :, :, 0]
                    step(tt(gt.rearrange("p (g k) -> p g k", k=2), sm.rearrange("p (g k) -> p g k", k=2), gate0, ALU.mult))
                    tt(p3, p3, gt.unsqueeze(2).to_broadcast([P, 8, 8]), ALU.mult).then_inc(probs_ready, 1)
                    for u in range(1, 10):
                        mask_unit(u)
                        norm_unit(u - 1)
                        collect(u - 3)
                    norm_unit(9)
                    for u in (7, 8, 9):
                        collect(u)

            def sample(l, hf):
                n = 2 * l + hf
                if hf == 0:
                    dve.wait_ge(rows_stored, 16 * 8 * (l + 1))
                for m in range(HALF * 2):
                    k = n * HALF * 2 + m
                    dve.wait_ge(bc_in[k % 2], 64 * (k // 2 + 1))
                    pages = bc_pages[:, k % 2, :, :]
                    tt(pages, pages, cmp_w[:, l, :].unsqueeze(1).to_broadcast([P, 4, 256]), ALU.mult).then_inc(bc_weighted, 1)
                b0 = SEQ + hf * HALF
                if hf == 0:
                    mark(nc.vector.memset(q_b[:, :], 0.0))
                    mark(nc.vector.memset(q_a[:, :], 0.0))
                    settle()
                for k in range(2):
                    half = slice(k * HD, (k + 1) * HD)
                    mark(copy(q_b[half, :].rearrange("p (b k) -> p b k", k=40)[:, :, k:k + 8:2],
                              feats[half, 4:8, b0:b0 + HALF].rearrange("p g b -> p b g")))
                    mark(copy(q_a[half, :].rearrange("p (b c k) -> p b c k", c=2, k=18)[:, :, :, k],
                              feats[half, 0:2, b0:b0 + HALF].rearrange("p c b -> p b c")))
                settle()
                dve.sem_inc(q_ready, 1)
                dve.wait_ge(bc_used, (n + 1) * HALF * 2)
                mark(copy(kcmp_s[:, :], banks[5][:, 0:P]))
                mark(copy(vcmp_s[0:CMP, :], banks[6][0:CMP, :]))
                settle()
                dve.sem_inc(cmp_out, 1)
                for b in range(HALF):
                    for i in (0, 2):
                        m = (n * HALF + b) * 4 + i
                        if m >= 4:
                            dve.wait_ge(kt_used, m - 3)
                        ps = bank_v()
                        free_v(copy(key_t[:, m % 4, :], ps[:, :]))
                dve.wait_ge(kt_used, 4 * HALF * (n + 1))
                st = s_stat[0:RB, :]
                misc = banks[4]
                step(ts(s_cmp[0:RB, :], misc[0:RB, 256:288], SCALE, None, ALU.mult))
                reduce(st[:, 0:1], s_cmp[0:RB, :], AX_X, ALU.max, negate=True).then_inc(s_masked, 1)
                mark(ts(s_win[0:RB, 0:512], banks[7][0:RB, :], SCALE, None, ALU.mult))
                mark(ts(s_win[0:RB, 512:513], misc[0:RB, 289:290], SCALE, None, ALU.mult))
                settle()
                reduce(st[:, 1:2], s_win[0:RB, :], AX_X, ALU.max, negate=True).then_inc(s_masked, 1)
                log_a = table_of("log_a", RA)
                mark(stt(s_a[0:RA, 0:256], misc[0:RA, 0:256], SCALE, log_a[:, 0:256], ALU.mult, ALU.add))
                mark(stt(s_a[0:RA, 256:257], misc[0:RA, 290:291], SCALE, log_a[:, 256:257], ALU.mult, ALU.add))
                settle()
                reduce(s_stat[0:RA, 2:3], s_a[0:RA, :], AX_X, ALU.max, negate=True).then_inc(s_masked, 1)
                ps = bank_v()
                free_v(tt(st[:, 16:40], ps[0:RB, 0:N_GATES], table_of("headmask", RB), ALU.mult))
                v_read()
                mark(reduce(st[:, 40:43], st[:, 16:40].rearrange("p (h t) -> p t h", t=3), AX_X, ALU.add))
                dve.wait_ge(s_exps, 4 * n + 1)
                step(nc.vector.reciprocal(st[:, 12:13], st[:, 8:9]))
                step(ts(s_cmp[0:RB, :], s_cmp[0:RB, :], st[:, 12:13], None, ALU.mult))
                dve.sem_inc(imp_ready, 1)
                ps = bank_v()
                imp, drop = st[:, 44:60], st[:, 60:76]
                free_v(reduce(imp, ps[0:RB, 0:CMP].rearrange("p (n t) -> p n t", t=2), AX_X, ALU.add))
                v_read()
                index = table_of("index", RB)
                step(reduce(st[:, 76:77], imp[:, 1:15], AX_X, ALU.min))
                step(nc.vector.memset(drop, 0.0))
                step(ts(drop[:, 1:15], imp[:, 1:15], st[:, 76:77], None, ALU.is_equal))
                step(tt(drop[:, 1:15], drop[:, 1:15], index, ALU.mult))
                step(reduce(st[:, 77:78], drop[:, 1:15], AX_X, ALU.max))
                step(ts(drop[:, 1:15], index, st[:, 77:78], MASKED, ALU.is_equal, ALU.mult))
                for i in range(2):
                    mark(stt(s_sel[0:RB, i * 512:(i + 1) * 512].rearrange("p (n k) -> p n k", n=8),
                             banks[5 + i][0:RB, :].rearrange("p (n k) -> p n k", n=8), SCALE,
                             drop[:, i * 8:(i + 1) * 8].unsqueeze(2).to_broadcast([RB, 8, HD]), ALU.mult, ALU.add))
                mark(ts(s_sel[0:RB, 1024:1025], misc[0:RB, 288:289], SCALE, None, ALU.mult))
                settle()
                reduce(st[:, 3:4], s_sel[0:RB, :], AX_X, ALU.max, negate=True).then_inc(s_masked, 1)
                dve.wait_ge(s_exps, 4 * n + 4)
                mark(nc.vector.reciprocal(st[:, 13:14], st[:, 9:10]))
                mark(nc.vector.reciprocal(s_stat[0:RA, 14:15], s_stat[0:RA, 10:11]))
                mark(nc.vector.reciprocal(st[:, 15:16], st[:, 11:12]))
                settle()
                mark(ts(s_cmp[0:RB, :], s_cmp[0:RB, :], st[:, 40:41], None, ALU.mult))
                mark(ts(s_sel[0:RB, :], s_sel[0:RB, :], st[:, 15:16], st[:, 41:42], ALU.mult, ALU.mult))
                mark(ts(s_win[0:RB, :], s_win[0:RB, :], st[:, 13:14], st[:, 42:43], ALU.mult, ALU.mult))
                mark(ts(s_a[0:RA, :], s_a[0:RA, :], s_stat[0:RA, 14:15], None, ALU.mult))
                settle()
                mine = table_of("own", RB)[:, hf * 8:hf * 8 + 8]
                mine_a = table_of("own_a", RA)[:, hf * 8:hf * 8 + 8]
                mark(ts(own_p[0:RB, 0:8], mine, s_sel[0:RB, 1024:1025], None, ALU.mult))
                mark(ts(own_p[0:RB, 8:16], mine, s_win[0:RB, 512:513], None, ALU.mult))
                mark(ts(own_p[0:RA, 16:24], mine_a, s_a[0:RA, 256:257], None, ALU.mult))
                settle()
                dve.sem_inc(s_probs, 1)
                ps = bank_v()
                copy(p_t[:, 0:384], ps[:, 0:384])
                copy(p_t[0:CMP, 384:416], ps[0:CMP, 384:416])
                free_v(copy(p_t[0:DEC, 416:480], ps[0:DEC, 416:480]))
                ps = bank_v()
                copy(p_t[:, 480:480 + 2 * RA], ps[:, 0:2 * RA])
                free_v(copy(p_t[0:DEC, 480 + 2 * RA:480 + 3 * RA], ps[0:DEC, 2 * RA:3 * RA]))
                v_read()
                dve.sem_inc(s_pt, 1)
                ps = bank_v(ring_used, HALF * (n + 1))
                for k in range(2):
                    half = slice(k * HD, (k + 1) * HD)
                    copy(mixed[half, 2:6, b0:b0 + HALF].rearrange("p g b -> p b g"),
                         ps[half, 0:RB].rearrange("p (b g k) -> p b g k", g=4, k=2)[:, :, :, k])
                    for c in range(2):
                        last = copy(mixed[half, c, b0:b0 + HALF],
                                    ps[half, RB + c * RA:RB + (c + 1) * RA].rearrange("p (b k) -> p b k", k=4)[:, :, 2 * c + k])
                free_v(last)

            for l in range(DEPTH):
                ffn(l, 0)
                mix(l)
                ffn(l, 1)
            for t in range(3):
                r, _, _ = rows_of(t)
                for half in range(2):
                    ps = bank_v()
                    free_v(copy(stage[0:r, t, half * 512:(half + 1) * 512], ps[0:r, :]))
                    v_read()
                    dve.sem_inc(stage_ready, 1)


_INS = ["x_prompt", "x_sample", "cache_a_kv", "cache_bc_kv", "cache_bs_kv", "cache_bw_kv", "state_c_h", "state_c_conv",
        "page_table", "w_in", "b_gate", "cmp_wk", "cmp_wv", "out_g_a", "out_g_b", "out_g_c", "conv_w", "conv_b",
        "lru_wr", "lru_br", "lru_wi", "lru_bi", "lru_lam", "w_out", "ln_g", "ln_b", "ffn_wg", "ffn_wu", "ffn_wd"]
_OUTS = [(1, 256, 1024), (8, 1, 1024), (2, 1, 256, 2, 4, 64), (2, 8, 1, 2, 4, 64),
         (2, 1, 2, 128, 2, 2, 64), (2, 8, 1, 2, 2, 64), (2, 1, 2, 128, 2, 2, 64), (2, 8, 1, 2, 2, 64),
         (2, 1, 256, 2, 2, 64), (2, 8, 1, 2, 2, 64), (2, 1, 256), (2, 8, 256), (2, 1, 3, 256), (2, 8, 3, 256)]


def shape_table():
    import numpy as np

    t = {n: np.zeros((P, b - a), np.float32) for n, (a, b) in TABLE.items()}
    p = np.arange(P)
    t["ident"][p, p] = 1.0
    t["mean"][:] = 1.0 / D_MODEL
    key = np.arange(SEQ)[None, :]
    for qb in range(2):
        q = (qb * P + p)[:, None]
        delta = q - key
        count = ((delta <= 128).astype(int) + (delta % 4 == 0) + (delta % 16 == 0)) * (delta >= 0)
        t["mask_a"][:, qb * SEQ:(qb + 1) * SEQ] = np.where(count > 0, np.log(np.maximum(count, 1)), MASKED)
        t["mask_c"][:, qb * SEQ:(qb + 1) * SEQ] = np.where(delta >= 0, 0.0, MASKED)
        vis = (np.arange(8) * CMP + CMP - 1)[None, :] <= q
        t["vis"][:, qb * 8:qb * 8 + 8] = vis
        t["vis_add"][:, qb * 8:qb * 8 + 8] = np.where(vis, 0.0, MASKED)
    half = HD // 2
    freq = (np.float32(10000.0) ** (-np.arange(half, dtype=np.float32) / np.float32(half))).astype(np.float32)
    for i, pos in enumerate((p, P + p, np.full(P, PAST))):
        ang = pos.astype(np.float32)[:, None] * freq[None, :]
        c, s = np.cos(ang), np.sin(ang)
        t["cos"][:, i * HD:(i + 1) * HD] = np.concatenate([c, c], 1)
        t["sin"][:, i * HD:(i + 1) * HD] = np.concatenate([-s, s], 1)
    t["sel4"][p, p // CMP] = 1.0
    t["selw"][p, 28 + p // CMP] = 1.0
    for tile in range(2):
        for h in range(8):
            t["selrep"][p, tile * HD + h * 8 + tile * 4 + p // CMP] = 1.0
    back = np.concatenate([P - p, 512 - 4 * np.arange(96), PAST - 16 * np.arange(32), [0]])
    count = (back <= 128).astype(int) + (back % 4 == 0) * (back <= 512) + (back % 16 == 0)
    t["log_a"][:] = np.log(count)[None, :]
    r = np.arange(RB)
    t["same"][:RB] = ((r[:, None] // 8 == r[None, :] // 8) & (r[:, None] % 2 == r[None, :] % 2))
    for hf in range(2):
        for b in range(DEC):
            t["expand"][b, hf * RB:(hf + 1) * RB] = (hf * HALF + r // 8) == b
            t["own"][:RB, hf * 8 + b] = (hf * HALF + r // 8) == b
            t["own_a"][:RA, hf * 8 + b] = (hf * HALF + np.arange(RA) // 4) == b
    for row in r:
        g, k = (row % 8) // 2, row % 2
        h = k * 4 + g
        t["headmask"][row, 3 * h:3 * h + 3] = 1.0
    t["index"][:] = np.arange(1, 15)[None, :]
    for hd in range(8):
        g, k = hd // 2, hd % 2
        t["maskv"][hd * 8:hd * 8 + 8, g * P + k * HD:g * P + (k + 1) * HD] = 1.0
    return np.concatenate([t[n] for n in TABLE], axis=1)


def kernel(**inputs):
    import numpy as _np
    import concourse.bacc as _bacc
    from concourse import mybir as _mybir
    from concourse.bass_utils import run_bass_kernel_spmd as _run

    nc = _bacc.Bacc("TRN2", target_bir_lowering=False, num_devices=1)
    arrays, args = {}, []
    for name in _INS + ["table"]:
        a = shape_table() if name == "table" else _np.ascontiguousarray(inputs[name])
        arrays[f"in_{name}_dram"] = a
        args.append(nc.dram_tensor(f"in_{name}_dram", a.shape, _mybir.dt.from_np(a.dtype), kind="ExternalInput").ap())
    for i, shape in enumerate(_OUTS):
        args.append(nc.dram_tensor(f"out_{i}_dram", shape, _mybir.dt.float32, kind="ExternalOutput").ap())
    build(nc, *args)
    r = _run(nc, [arrays], core_ids=[0])
    return tuple(r.results[0][f"out_{i}_dram"] for i in range(len(_OUTS)))
```

```python
from contextlib import ExitStack

import concourse.bass as bass
from concourse import mybir

P = 128
D_MODEL = 1024
SEQ = 256
DEPTH = 2
DEC = 8
PAST = 1024
PAGE = 128
PAGES = PAST // PAGE
HD = 64
D_FF = 2816
CMP = 32
C_WIDTH = 256
ALPHA = (2 * DEPTH) ** 0.25
EPS = 1e-5
SCALE = HD ** -0.5
LRU_C = 8.0
MASKED = -1e30
SPLIT = 6
LOG_OWN = 1.0986122886681098

TOK = SEQ + DEC
KC = D_MODEL // P
FC = D_FF // P
TT = SEQ // P
N_TOKEN_MAJOR = 2048
N_GATES = 24
C_COL = N_TOKEN_MAJOR + N_GATES

AQ, AK, AV, BQ, BC, BS, BW = 0, 256, 512, 768, 1280, 1536, 1792

SLOTS = 3
SLOT = 4096
GROUP = 256
FFN_GROUPS = D_FF // GROUP
FFN_USES = FFN_GROUPS + KC
MIX_USES = 5 + 2
LAYER_USES = 2 * FFN_USES + MIX_USES
assert LAYER_USES % SLOTS == 0
WIN_USE, WOUT_USE = FFN_USES, FFN_USES + 5
LOOPED = FFN_GROUPS // SLOTS

HALF = DEC // 2
RING = HALF
RING_W = PAGES * 256 + 4 * 256 + 2 * 512
RB, RA = HALF * 8, HALF * 4
N_SEL = PAST + 1
N_WIN = 512 + 1
N_A = 256 + 1

ALU = mybir.AluOpType
ACT = mybir.ActivationFunctionType
F32 = mybir.dt.float32
I32 = mybir.dt.int32
AX_X = mybir.AxisListType.X

V_START = KC + DEPTH
V_LAYER = 2 + 12 + 1 + 3 + 5 + 1 + 1 + 2 * (2 * HALF + 3 + 3)
A_LAYER = 2 + 4 + 5 + 2 * (1 + 10) + 2 * 2 * HALF

TABLE = {}
TABLE_COLS = 0
for _name, _cols in (("ident", P), ("mean", P), ("mask_a", 2 * SEQ), ("mask_c", 2 * SEQ), ("vis_add", 16),
                     ("vis", 16), ("cos", 3 * HD), ("sin", 3 * HD), ("sel4", 4), ("selw", 60), ("selrep", 2 * HD),
                     ("log_a", N_A), ("same", RB), ("expand", 2 * RB), ("headmask", N_GATES),
                     ("index", 14), ("own", 16), ("own_a", 16), ("own4", HALF), ("maskv", 512)):
    TABLE[_name] = (TABLE_COLS, TABLE_COLS + _cols)
    TABLE_COLS += _cols


def landed_counts():
    dmas = [2] * LAYER_USES
    dmas[WOUT_USE] = dmas[WOUT_USE + 1] = 4
    total, out = [0] * SLOTS, []
    for k, n in enumerate(dmas):
        total[k % SLOTS] += 16 * n
        out.append(total[k % SLOTS])
    return out, total


class Tally:

    def __init__(self):
        self.n = {}

    def next(self, sem, by=1):
        self.n[sem] = self.n.get(sem, 0) + by
        return self.n[sem]

    def now(self, sem):
        return self.n.get(sem, 0)


def build(nc, x_prompt, x_sample, cache_a_kv, cache_bc_kv, cache_bs_kv, cache_bw_kv, state_c_h, state_c_conv,
          page_table, w_in, b_gate, cmp_wk, cmp_wv, out_g_a, out_g_b, out_g_c, conv_w, conv_b, lru_wr, lru_br,
          lru_wi, lru_bi, lru_lam, w_out, ln_g, ln_b, ffn_wg, ffn_wu, ffn_wd, table,
          y_prompt, y_sample, a_prompt, a_sample, bc_prompt, bc_sample, bs_prompt, bs_sample, bw_prompt, bw_sample,
          h_prompt, h_sample, conv_prompt, conv_sample):
    n_pool = cache_bc_kv.shape[1]
    ctx = ExitStack()
    with ctx:
        def sb(name, shape, dt=F32):
            return ctx.enter_context(nc.sbuf_tensor(name, shape, dt))

        names = {}

        def sem(name):
            return ctx.enter_context(nc.semaphore(name))

        consts = sb("consts", [P, TABLE_COLS])
        weights = sb("weights", [P, SLOTS, SLOT])
        ring = sb("ring", [P, RING, RING_W])
        x = sb("x", [P, KC, TOK])
        z = sb("z", [P, KC, TOK])
        bc_pages = sb("bc_pages", [P, 2, 4, 256])
        params = sb("params", [P, DEPTH, 72])
        states = sb("states", [P, DEPTH, 64])
        cmp_w = sb("cmp_w", [P, DEPTH, 256])
        gate_bias = sb("gate_bias", [P, DEPTH, N_GATES])
        gate_w = sb("gate_w", [P, KC, N_GATES])
        lru_w = sb("lru_w", [P, 4, P])
        decay = sb("decay", [P, DEPTH, 2])
        eps = sb("eps", [P, 2])
        mean_sb = sb("mean_sb", [P, TOK])
        rstd = sb("rstd", [P, 3, TOK])
        warm = sb("warm", [P, 1])
        pt_sb = sb("pt_sb", [1, DEC * PAGES], I32)
        shared = sb("shared", [P, 12560])
        at = [0]

        def carve(cols, reset=None):
            if reset is not None:
                at[0] = reset
            a = at[0]
            at[0] += cols
            assert at[0] <= 12560, at[0]
            return shared[:, a:a + cols]

        hidden = carve(FC * TOK, 0).rearrange("p (c t) -> p c t", c=FC)
        silu = carve(2 * TOK).rearrange("p (c t) -> p c t", c=2)
        tokens = carve(TT * 2048, 0).rearrange("p (t n) -> p t n", t=TT)
        feats = carve(10 * TOK).rearrange("p (c t) -> p c t", c=10)
        mixed = carve(KC * TOK).rearrange("p (c t) -> p c t", c=KC)
        squares = carve(2 * TOK).rearrange("p (c t) -> p c t", c=2)
        gates = carve(3 * N_GATES).rearrange("p (t n) -> p t n", t=3)
        scratch = at[0]
        rope_t = carve(2 * 512).rearrange("p (t n) -> p t n", t=2)
        conv_x = carve(2 * 260).rearrange("p (c t) -> p c t", c=2)
        conv_s = carve(2 * DEC * 4).rearrange("p (c b j) -> p c b j", c=2, b=DEC)
        gelu = carve(2 * TOK).rearrange("p (c t) -> p c t", c=2)
        lru_i = feats[:, 0:2, :]
        xc, lru_r, lru_t = mixed[:, 0:2, :], mixed[:, 2:4, :], mixed[:, 4:6, :]
        probs = carve(3 * 512, scratch).rearrange("p (r b n) -> p r b n", r=3, b=2)
        probs_t = carve(2 * 512).rearrange("p (r n) -> p r n", r=2)
        prod_c = probs_t
        stat = carve(4 * 8).rearrange("p (r n) -> p r n", r=4)
        finals_t = carve(256)
        vcmp = squares[:, :, :].rearrange("p c t -> p (c t)")[:, 0:512]
        pc_t, pc, kcmp, pc_stat = mean_sb[:, 0:128], mean_sb[:, 128:192], mean_sb[:, 192:200], mean_sb[:, 200:224]
        finals = probs_t[:, 1, 128:200].rearrange("p (c t) -> p c t", c=2)
        assert (WIN_USE + 4) % SLOTS == (WOUT_USE + 2) % SLOTS == SLOTS - 1
        spare = [0]

        def carve_slot(cols):
            a = spare[0]
            spare[0] += cols
            assert spare[0] <= SLOT, spare[0]
            return weights[:, SLOTS - 1, a:a + cols]

        key_t = carve_slot(4 * 512).rearrange("p (e n) -> p e n", e=4)
        outs = key_t[0:8, 0:3, :]
        kcmp_rows = key_t[:, 0, 0:256].rearrange("p (h n) -> p h n", h=2)
        s_sel, s_win, s_a, s_cmp = carve_slot(N_SEL), carve_slot(N_WIN), carve_slot(N_A), carve_slot(CMP)
        s_cmp4, s_stat = carve_slot(P), carve_slot(80)
        q_a, kcmp_s = tokens[:, 0, 0:144], tokens[:, 1, 0:256]
        q_b, vcmp_s = tokens[:, 0, BQ:BQ + 160], tokens[:, 0, BQ + 160:BQ + 416]
        own_p = tokens[:, 1, BQ:BQ + 24]
        p_t = rstd[:, :, :].rearrange("p g t -> p (g t)")[:, 0:560]
        stage = carve(3 * D_MODEL, 0).rearrange("p (t n) -> p t n", t=3)
        rows = carve(2 * DEPTH * P, 6400).rearrange("p (l n) -> p l n", l=2 * DEPTH)
        z_flat = z[:, :, :].rearrange("p c t -> p (c t)")
        samples = z_flat[0:DEC, 0:2048]

        def table_of(name, rows_=P):
            a, b = TABLE[name]
            return consts[0:rows_, a:b]

        ident = table_of("ident")
        mean_w = table_of("mean")

        def slot(k):
            return weights[:, k % SLOTS, :]

        def rows_of(t):
            if t < TT:
                return P, slice(t * P, (t + 1) * P), tokens[:, t, :]
            return DEC, slice(SEQ, TOK), samples

        banks = [ctx.enter_context(nc.psum_tensor(f"bank{i}", [P, 512], F32)) for i in range(8)]

        consts_in, x_in, rows_in, page_in = sem("consts_in"), sem("x_in"), sem("rows_in"), sem("page_in")
        small_in, gate_w_in, lru_w_in = sem("small_in"), sem("gate_w_in"), sem("lru_w_in")
        landed = [sem(f"landed{i}") for i in range(SLOTS)]
        ring_in = [sem(f"ring_in{i}") for i in range(RING)]
        ring_used = sem("ring_used")
        bc_in = [sem(f"bc_in{i}") for i in range(2)]
        bc_weighted, bc_used = sem("bc_weighted"), sem("bc_used")
        cleared, warm_ready = sem("cleared"), sem("warm_ready")
        v_full, v_free = sem("v_full"), sem("v_free")
        a_full, a_free = sem("a_full"), sem("a_free")
        s_full, s_free = sem("s_full"), sem("s_free")
        gate_full, up_full, silu_done, hidden_done = sem("gate_full"), sem("up_full"), sem("silu_done"), sem("hidden_done")
        y_full, z_done, sq_done, stat_done = sem("y_full"), sem("z_done"), sem("sq_done"), sem("stat_done")
        var_done, std_done, norm_done, x_ready = sem("var_done"), sem("std_done"), sem("norm_done"), sem("x_ready")
        tok_ready, gates_raw, gates_ready = sem("tok_ready"), sem("gates_raw"), sem("gates_ready")
        xc_ready, gate_r, lru_f, lru_s, gelu_ready, finals_ready = (
            sem("xc_ready"), sem("lru_gates"), sem("lru_f"), sem("lru_s"), sem("gelu_ready"), sem("finals_ready"))
        prod_ready, cmp_ready, masked, exps, probs_ready, pv_done = (
            sem("prod_ready"), sem("cmp_ready"), sem("masked"), sem("exps"), sem("probs_ready"), sem("pv_done"))
        mix_ready = sem("mix_ready")
        q_ready, cmp_full, cmp_out = sem("q_ready"), sem("cmp_full"), sem("cmp_out")
        kt_used = sem("kt_used")
        s_masked, s_exps, imp_ready, s_probs, s_pt, outs_ready, musq_done, sub_done, mean_done = (
            sem("s_masked"), sem("s_exps"), sem("imp_ready"), sem("s_probs"), sem("s_pt"),
            sem("outs_ready"), sem("musq_done"), sem("sub_done"), sem("mean_done"))
        rms_sq, rms_stat, rms_var, rms_std, yn_ready = sem("rms_sq"), sem("rms_stat"), sem("rms_var"), sem("rms_std"), sem("yn_ready")
        vec, act_own = sem("vector_step"), sem("scalar_step")
        stage_ready, rows_stored, states_stored, y_stored = (
            sem("stage_ready"), sem("rows_stored"), sem("states_stored"), sem("y_stored"))
        state_ready = sem("state_ready")

        landed_at, landed_layer = landed_counts()

        def landed_value(l, k):
            return l * landed_layer[k % SLOTS] + landed_at[k]

        block = ctx.enter_context(nc.Block())

        @block.sync
        def _(sp):
            bc_count, ring_count = [0], [0]
            sp.dma_start(pt_sb[:, :], page_table.rearrange("b p -> (b p)").unsqueeze(0)).then_inc(page_in, 16)
            sp.dma_start(stage[:, 0:TT, :], x_prompt[0].rearrange("(t p) d -> p t d", p=P)).then_inc(x_in, 16)
            sp.dma_start(stage[0:DEC, TT, :], x_sample.rearrange("b s d -> (b s) d")).then_inc(x_in, 16)
            sp.dma_start(consts[:, :], table).then_inc(consts_in, 16)
            sp.wait_ge(page_in, 16)

            def used(l, k):
                if k < 0:
                    l, k = l - 1, k + LAYER_USES
                if k == WIN_USE:
                    return a_full, l * A_LAYER + 2
                if k <= WIN_USE + 4 and k > WIN_USE:
                    return v_full, V_START + l * V_LAYER + (5, 8, 11, 15)[k - WIN_USE - 1]
                if k in (WOUT_USE, WOUT_USE + 1):
                    return y_full, (3 * l + 1) * KC + 4 * (k - WOUT_USE + 1)
                j = k > WOUT_USE
                g = k - (WOUT_USE + 2) * j
                if g < FFN_GROUPS:
                    return up_full, (2 * l + j) * FC + 2 * (g + 1)
                return y_full, (3 * l + 2 * j) * KC + g - FFN_GROUPS + 1

            def load_slot(l, k, parts):
                if l * LAYER_USES + k >= SLOTS:
                    sp.wait_ge(*used(l, k - SLOTS))
                for dst, src in parts:
                    sp.dma_start(dst, src).then_inc(landed[k % SLOTS], 16)

            def ffn_parts(l, j, k, col):
                dst = slot(k).rearrange("p (w c f) -> p w c f", w=2, c=KC)
                return [(dst[:, i, :, :], w[l, j].rearrange("(c p) f -> p c f", p=P)[:, :, col])
                        for i, w in enumerate((ffn_wg, ffn_wu))]

            def load_ring(l, b):
                n = ring_count[0]
                s = n % RING
                ring_count[0] += 1
                if n >= RING:
                    sp.wait_ge(ring_used, n - RING + 1)
                for p in range(PAGES):
                    page = sp.value_load(pt_sb[0:1, b * PAGES + p:b * PAGES + p + 1], min_val=0, max_val=n_pool - 1)
                    sp.dma_start(ring[:, s, p * 256:(p + 1) * 256],
                                 cache_bs_kv[l, bass.ds(page, 1)].rearrange("o r a h d -> (o r) (a h d)"))\
                        .then_inc(ring_in[s], 16)
                sp.dma_start(ring[:, s, 2048:3072].rearrange("p (t n) -> p t n", t=4),
                             cache_bw_kv[l, b].rearrange("(t p) a h d -> p t (a h d)", p=P)).then_inc(ring_in[s], 16)
                rows_a = cache_a_kv[l, b].rearrange("r a h d -> r (a h d)")
                sp.dma_start(ring[:, s, 3072:3584], rows_a[PAST - P:PAST, :]).then_inc(ring_in[s], 16)
                sp.dma_start(ring[0:96, s, 3584:4096],
                             rows_a[512:896, :].rearrange("(p s) n -> p s n", s=4)[:, 0, :]).then_inc(ring_in[s], 16)
                sp.dma_start(ring[96:P, s, 3584:4096],
                             rows_a[0:512, :].rearrange("(p s) n -> p s n", s=16)[:, 0, :]).then_inc(ring_in[s], 16)

            def load_bc(l, b, part):
                n = bc_count[0]
                bc_count[0] += 1
                if n >= 2:
                    sp.wait_ge(bc_used, n - 1)
                for i in range(4):
                    p = part * 4 + i
                    page = sp.value_load(pt_sb[0:1, b * PAGES + p:b * PAGES + p + 1], min_val=0, max_val=n_pool - 1)
                    sp.dma_start(bc_pages[:, n % 2, i, :],
                                 cache_bc_kv[l, bass.ds(page, 1)].rearrange("o r a h d -> (o r) (a h d)"))\
                        .then_inc(bc_in[n % 2], 16)

            def ffn(l, j, base, extra):
                first = 2 if extra else 1
                for g in range(first * SLOTS):
                    load_slot(l, base + g, ffn_parts(l, j, base + g, slice(g * GROUP, (g + 1) * GROUP)))
                    if extra:
                        extra(g)
                with sp.Fori(first, LOOPED) as i:
                    for s in range(SLOTS):
                        sp.wait_ge(up_full, (2 * l + j) * FC + 2 * (s - SLOTS + 1) + i * (2 * SLOTS))
                        for dst, src in ffn_parts(l, j, base + s, bass.ds(i * (SLOTS * GROUP) + s * GROUP, GROUP)):
                            sp.dma_start(dst, src).then_inc(landed[(base + s) % SLOTS], 16)
                for g in range(LOOPED * SLOTS, FFN_GROUPS):
                    load_slot(l, base + g, ffn_parts(l, j, base + g, slice(g * GROUP, (g + 1) * GROUP)))
                wd = ffn_wd[l, j].rearrange("(c p) d -> p c d", p=P)
                for g in range(KC):
                    k = base + FFN_GROUPS + g
                    dst = slot(k)[:, 0:FC * P].rearrange("p (c d) -> p c d", c=FC)
                    load_slot(l, k, [(dst[:, a:a + FC // 2, :], wd[:, a:a + FC // 2, g * P:(g + 1) * P])
                                     for a in (0, FC // 2)])

            for l in range(DEPTH):
                def behind(g, l=l):
                    if g < HALF:
                        load_ring(l, g)

                ffn(l, 0, 0, behind)
                w = w_in[l].rearrange("(c p) n -> p c n", p=P)

                def load_w_in(g):
                    col = slice((g - 1) * 512, g * 512) if g else slice(C_COL, C_COL + 512)
                    dst = slot(WIN_USE + g).rearrange("p (c n) -> p c n", c=KC)
                    load_slot(l, WIN_USE + g, [(dst[:, a:a + 4, :], w[:, a:a + 4, col]) for a in (0, 4)])

                def load_pages(a, b):
                    for m in range(a, b):
                        load_bc(l, m // 2, m % 2)

                load_pages(0, 2)
                load_w_in(0)
                if l:
                    sp.wait_ge(v_full, V_START + (l - 1) * V_LAYER + 18)
                sp.dma_start(gate_w[:, :, :], w[:, :, N_TOKEN_MAJOR:C_COL]).then_inc(gate_w_in, 16)
                load_w_in(1)
                load_w_in(2)
                load_pages(2, 5)
                load_w_in(3)
                load_pages(5, 8)
                load_w_in(4)
                load_pages(8, 2 * DEC)
                wo = w_out[l]
                for g in range(2):
                    dst = slot(WOUT_USE + g).rearrange("p (c n) -> p c n", c=KC)
                    col = slice(g * 512, (g + 1) * 512)
                    rows_b = wo[256:768, col].rearrange("(k g d) n -> k d g n", k=2, g=4)
                    load_slot(l, WOUT_USE + g, [
                        (dst[:, 0:2, :], wo[0:256, col].rearrange("(c p) n -> p c n", p=P)),
                        (dst[0:HD, 2:6, :], rows_b[0]), (dst[HD:P, 2:6, :], rows_b[1]),
                        (dst[:, 6:8, :], wo[768:1024, col].rearrange("(c p) n -> p c n", p=P))])
                for b in range(HALF, DEC):
                    load_ring(l, b)
                sp.wait_ge(mix_ready, l + 1)
                ffn(l, 1, WOUT_USE + 2, None)

        @block.gpsimd
        def _(pool):
            pool.memset(lru_w[:, :, :], 0.0).then_inc(cleared, 1)
            pool.memset(warm[:, :], 1.0).then_inc(warm_ready, 1)
            seen = Tally()
            for l in range(DEPTH):
                r0, r1 = rows[:, 2 * l, :], rows[:, 2 * l + 1, :]
                for at_, src in ((0, ln_g[l].rearrange("i (c p) -> (i c) p", p=P)),
                                 (24, ln_b[l].rearrange("i (c p) -> (i c) p", p=P)),
                                 (48, out_g_a[l].rearrange("(c p) -> c p", p=P)),
                                 (54, out_g_c[l].rearrange("(c p) -> c p", p=P)),
                                 (56, conv_w[l].rearrange("j (c p) -> (j c) p", p=P)),
                                 (64, conv_b[l].rearrange("(c p) -> c p", p=P)),
                                 (66, lru_br[l].rearrange("(c p) -> c p", p=P)),
                                 (68, lru_bi[l].rearrange("(c p) -> c p", p=P)),
                                 (70, lru_lam[l].rearrange("(c p) -> c p", p=P))):
                    pool.dma_start(r0[at_:at_ + src.shape[0], :], src).then_inc(rows_in, 16)
                gb = out_g_b[l].rearrange("(k g d) -> k g d", k=2, g=4)
                for k in range(2):
                    pool.dma_start(r0[50:54, k * HD:(k + 1) * HD], gb[k]).then_inc(rows_in, 16)
                for c in range(2):
                    pool.dma_start(r1[c * 24:c * 24 + 24, :],
                                   state_c_conv[l].rearrange("b j n -> (b j) n")[:, c * P:(c + 1) * P]).then_inc(rows_in, 16)
                    pool.dma_start(r1[48 + c * 8:56 + c * 8, :], state_c_h[l][:, c * P:(c + 1) * P]).then_inc(rows_in, 16)
            for l in range(DEPTH):
                for n in range(4):
                    for kv, w in enumerate((cmp_wk, cmp_wv)):
                        for h in range(2):
                            o = kv * P + h * HD
                            pool.dma_start(cmp_w[n * CMP:(n + 1) * CMP, l, o:o + HD], w[l]).then_inc(small_in, 16)
                pool.dma_start(gate_bias[:, l, :], b_gate[l].unsqueeze(0).to_broadcast([P, N_GATES])).then_inc(small_in, 16)

            def subtract_mean(n):
                pool.wait_ge(mean_done, n + 1)
                for c in range(KC):
                    nc.gpsimd.tensor_tensor(z[:, c, :], z[:, c, :], mean_sb[:, :], ALU.subtract).then_inc(sub_done, 1)

            for l in range(DEPTH):
                if l:
                    pool.wait_ge(finals_ready, l)
                else:
                    pool.wait_ge(cleared, 1)
                for n in range(4):
                    a, c = (n % 2) * HD, n // 2
                    for i, w in enumerate((lru_wr, lru_wi)):
                        pool.dma_start(lru_w[a:a + HD, c * 2 + i, a:a + HD], w[l, n]).then_inc(lru_w_in, 16)
                subtract_mean(3 * l)
                pool.wait_ge(state_ready, l + 1)
                pool.dma_start(h_prompt[l], finals_t[0:1, :]).then_inc(states_stored, 16)
                pool.dma_start(h_sample[l], finals_t[1:9, :]).then_inc(states_stored, 16)
                pool.dma_start(conv_prompt[l, 0], finals_t[9:12, :]).then_inc(states_stored, 16)
                pool.dma_start(conv_sample[l].rearrange("b j n -> (b j) n"), finals_t[12:36, :]).then_inc(states_stored, 16)
                pool.wait_ge(tok_ready, (l + 1) * 12)
                for col, width, out_p, out_s in ((AK, 512, a_prompt, a_sample), (BC, 256, bc_prompt, bc_sample),
                                                 (BS, 256, bs_prompt, bs_sample), (BW, 256, bw_prompt, bw_sample)):
                    if len(out_p.shape) == 7:
                        dst = out_p[l, 0].rearrange("g r a h d -> r g (a h d)")
                    else:
                        dst = out_p[l, 0].rearrange("(t r) a h d -> r t (a h d)", r=P)
                    pool.dma_start(dst, tokens[:, :, col:col + width]).then_inc(rows_stored, 16)
                    pool.dma_start(out_s[l, :, 0].rearrange("b a h d -> b (a h d)"),
                                   samples[:, col:col + width]).then_inc(rows_stored, 16)
                subtract_mean(3 * l + 1)
                subtract_mean(3 * l + 2)
            pool.wait_ge(stage_ready, 6)
            pool.dma_start(y_prompt[0].rearrange("(t p) d -> p t d", p=P), stage[:, 0:TT, :]).then_inc(y_stored, 16)
            pool.dma_start(y_sample.rearrange("b s d -> (b s) d"), stage[0:DEC, TT, :]).then_inc(y_stored, 16)
            pool.wait_ge(rows_stored, 16 * 8 * DEPTH)
            pool.wait_ge(states_stored, 16 * 4 * DEPTH)
            pool.wait_ge(y_stored, 32)

        @block.tensor
        def _(pe):
            seen, made = Tally(), Tally()

            def bank_v():
                n = made.next("v tiles")
                if n > 2:
                    pe.wait_ge(v_free, n - 2)
                return banks[(n - 1) % 2]

            def bank_a():
                n = made.next(a_full)
                if n > 2:
                    pe.wait_ge(a_free, n - 2)
                return banks[2 + (n - 1) % 2]

            def bank_s():
                n = made.next(s_full)
                if n > 3:
                    pe.wait_ge(s_free, n - 3)
                return banks[5 + (n - 1) % 3]

            mm = nc.tensor.matmul

            def part(*a, **k):
                return mm(*a, skip_group_check=True, **k)

            pe.wait_ge(consts_in, 16)
            pe.wait_ge(x_in, 32)
            for c in range(KC):
                out = bank_v()
                for t in range(3):
                    r, col, _ = rows_of(t)
                    last = nc.tensor.transpose(out[:, col], stage[0:r, t, c * P:(c + 1) * P], ident[0:r, 0:r])
                last.then_inc(v_full, 1)

            def turn_rows():
                pe.wait_ge(rows_in, 16 * 15 * DEPTH)
                for l in range(DEPTH):
                    out = bank_v()
                    nc.tensor.transpose(out[:, 0:72], rows[0:72, 2 * l, :], ident[0:72, 0:72])
                    nc.tensor.transpose(out[:, 128:192], rows[0:64, 2 * l + 1, :], ident[0:64, 0:64]).then_inc(v_full, 1)

            def wait_x(l, phase, c=KC - 1):
                pe.wait_ge(x_ready, KC * (3 * l + phase) + c + 1)

            def ffn(l, j, base):
                f = 2 * l + j
                pe.wait_ge(v_free, made.now("v tiles"))

                def group(k, value, n0):
                    w = slot(k).rearrange("p (w c f) -> p w c f", w=2, c=KC)
                    pe.wait_ge(landed[k % SLOTS], value)
                    for q in range(2):
                        if not isinstance(n0, int) or f or n0 + q >= 2:
                            pe.wait_ge(hidden_done, n0 + (f * FC + q - 1))
                        for i, full in ((0, gate_full), (1, up_full)):
                            for c in range(KC):
                                if isinstance(n0, int) and n0 + q + i == 0:
                                    wait_x(l, 2 * j, c)
                                last = mm(banks[2 * q + i][:, 0:TOK], w[:, i, c, q * P:(q + 1) * P], x[:, c, :],
                                          start=(c == 0), stop=(c == KC - 1))
                            last.then_inc(full, 1)

                for g in range(SLOTS):
                    group(base + g, landed_value(l, base + g), 2 * g)
                with pe.Fori(1, LOOPED) as i:
                    for s in range(SLOTS):
                        group(base + s, landed_value(l, base + s) + i * 32, i * (2 * SLOTS) + 2 * s)
                for g in range(LOOPED * SLOTS, FFN_GROUPS):
                    group(base + g, landed_value(l, base + g), 2 * g)

                def down(g):
                    k = base + FFN_GROUPS + g
                    w = slot(k)[:, 0:FC * P].rearrange("p (c d) -> p c d", c=FC)
                    pe.wait_ge(landed[k % SLOTS], landed_value(l, k))
                    return w

                pe.wait_ge(hidden_done, (f + 1) * FC)
                if f == 0:
                    turn_rows()
                residual(3 * l + 2 * j, down, lambda w, c, g: w[:, c, :], hidden, FC)

            def residual(n, weights_of, pick, source, chunks):
                def stats(g):
                    pe.wait_ge(sq_done, n * KC + g + 1)
                    mm(banks[6][:, 0:TOK], mean_w, z[:, g, :], start=(g == 0), stop=(g == KC - 1), skip_group_check=True)
                    mm(banks[7][:, 0:TOK], mean_w, squares_ffn(g), start=(g == 0), stop=(g == KC - 1),
                       skip_group_check=True).then_inc(stat_done, 1)

                for g in range(KC):
                    w = weights_of(g)
                    if g >= 2:
                        pe.wait_ge(z_done, n * KC + g - 1)
                    for c in range(chunks):
                        last = mm(banks[4 + g % 2][:, 0:TOK], pick(w, c, g), source[:, c, :],
                                  start=(c == 0), stop=(c == chunks - 1))
                    last.then_inc(y_full, 1)
                    if g:
                        stats(g - 1)
                stats(KC - 1)

            def mix(l):
                compressed = [0]

                def compress():
                    m = compressed[0]
                    compressed[0] += 1
                    b, half = m // 2, m % 2
                    pe.wait_ge(bc_weighted, l * 2 * DEC + m + 1)
                    for i in range(4):
                        page = half * 4 + i
                        row = (b % HALF) * CMP
                        last = part(banks[4][row:row + CMP, (b // HALF) * 256:(b // HALF + 1) * 256],
                                    table_of("selw")[:, 28 - 4 * page:60 - 4 * page], bc_pages[:, m % 2, i, :],
                                    start=(page == 0), stop=(page == 7))
                    last.then_inc(bc_used, 1)

                k = WIN_USE
                w = slot(k).rearrange("p (c n) -> p c n", c=KC)
                pe.wait_ge(landed[k % SLOTS], landed_value(l, k))
                for m in range(4):
                    out = bank_v() if m < 2 else bank_a()
                    for c in range(KC):
                        if m == 0:
                            wait_x(l, 1, c)
                        last = mm(out[:, 0:TOK], w[:, c, m * P:(m + 1) * P], x[:, c, :], start=(c == 0), stop=(c == KC - 1))
                    last.then_inc(v_full if m < 2 else a_full, 1)
                for g in range(4):
                    k = WIN_USE + 1 + g
                    w = slot(k).rearrange("p (c n) -> p c n", c=KC)
                    pe.wait_ge(landed[k % SLOTS], landed_value(l, k))
                    for t in range(3):
                        r, col, _ = rows_of(t)
                        out = bank_v()
                        for c in range(KC):
                            last = mm(out[0:r, :], x[:, c, col], w[:, c, :], start=(c == 0), stop=(c == KC - 1))
                        last.then_inc(v_full, 1)
                        compress()
                    if g == 0:
                        pe.wait_ge(lru_w_in, 16 * 8 * (l + 1))
                        pe.wait_ge(xc_ready, l + 1)
                        for c in range(2):
                            for i in range(2):
                                out = bank_a()
                                mm(out[:, 0:TOK], lru_w[:, c * 2 + i, :], xc[:, c, :], start=True, stop=True)\
                                    .then_inc(a_full, 1)
                    if g == 2:
                        pe.wait_ge(finals_ready, l + 1)
                        out = bank_v()
                        nc.tensor.transpose(out[0:36, 0:P], finals[:, 0, :], ident)
                        nc.tensor.transpose(out[0:36, P:2 * P], finals[:, 1, :], ident).then_inc(v_full, 1)
                        compress()
                pe.wait_ge(gate_w_in, 16 * (l + 1))
                for t in range(3):
                    r, col, _ = rows_of(t)
                    out = bank_v()
                    for c in range(KC):
                        last = mm(out[0:r, 0:N_GATES], x[:, c, col], gate_w[:, c, :], start=(c == 0), stop=(c == KC - 1))
                    last.then_inc(v_full, 1)
                    compress()
                pe.wait_ge(tok_ready, 12 * (l + 1))
                for n, col_t in enumerate((AQ, AQ + P, AK, AK + P, BQ, BQ + P, BQ + 2 * P, BQ + 3 * P, BS, BW)):
                    out = bank_v() if n % 2 else bank_a()
                    for t in range(3):
                        r, col, src = rows_of(t)
                        last = nc.tensor.transpose(out[:, col], src[:, col_t:col_t + P], ident[0:r, 0:r])
                    last.then_inc(v_full if n % 2 else a_full, 1)
                feats_tiles[:] = made.now(a_full), made.now("v tiles")
                prompt_start(l)
                sample_scores(l, 0)
                prompt_block(l, 0, 0, 10)
                sample_values(l, 0)
                prompt_block(l, 1, 0, SPLIT)
                sample_scores(l, 1)
                prompt_block(l, 1, SPLIT, 10)
                sample_values(l, 1)
                for c in range(KC):
                    pe.wait_ge(rms_sq, l * KC + c + 1)
                    g = 0 if c < 2 else 1 if c < 6 else 2
                    mm(banks[4 + g][:, 0:TOK], mean_w, squares[:, c % 2, :], start=c in (0, 2, 6), stop=c in (1, 5, 7))\
                        .then_inc(rms_stat, 1)
                pe.wait_ge(yn_ready, KC * (l + 1))

                def weights_of(g):
                    k = WOUT_USE + g // 4
                    if g % 4 == 0:
                        pe.wait_ge(landed[k % SLOTS], landed_value(l, k))
                    return slot(k).rearrange("p (c n) -> p c n", c=KC)

                residual(3 * l + 1, weights_of, lambda w, c, g: w[:, c, (g % 4) * P:(g % 4 + 1) * P], mixed, KC)

            feats_tiles = [0, 0]
            opened = [None]

            def prompt_start(l):
                pe.wait_ge(a_free, feats_tiles[0])
                pe.wait_ge(v_free, feats_tiles[1])
                pe.wait_ge(prod_ready, l + 1)
                out = bank_v()
                for t in range(TT):
                    part(out[:, 4 * t:4 * t + 4], prod_c[:, t, 0:P], table_of("sel4"), start=(t == 0), stop=False)
                rep = table_of("selrep").rearrange("p (t n) -> p t n", t=TT)
                for t in range(TT):
                    last = part(out[0:HD, P:2 * P], rep[:, t, :], prod_c[:, t, P:2 * P], start=False, stop=(t == 1))
                last.then_inc(v_full, 1)
                pe.wait_ge(cmp_out, l + 1)
                out = bank_v()
                for hf in range(2):
                    last = nc.tensor.transpose(out[:, hf * P:(hf + 1) * P], kcmp_rows[:, hf, :], ident)
                last.then_inc(v_full, 1)
                pe.wait_ge(cmp_ready, l + 1)

            def prompt_block(l, qb, ua, ub):
                    pe.wait_ge(s_masked, 4 * (2 * l + (2 if ua else 1)))
                    q_cols = slice(qb * P, (qb + 1) * P)
                    nk = (qb + 1) * P
                    done = l * 2 * 10 + qb * 10

                    def scores(u):
                        out = bank_s()[:, :].rearrange("p (b n) -> p b n", b=2)
                        for i in range(2):
                            if u < 2:
                                a, q, key = u * HD, i, 2 + i
                            else:
                                a, q, key = ((u - 2) % 2) * HD, 4 + (u - 2) // 2, 8 + i
                            last = part(out[:, i, 0:nk], feats[a:a + HD, q, q_cols], feats[a:a + HD, key, 0:nk],
                                        start=(i == 0), stop=(i == 1))
                        last.then_inc(s_full, 1)

                    def turn(u):
                        pe.wait_ge(probs_ready, done + u + 1 + (2 * l + qb + 1))
                        out = bank_a()
                        for i in range(2):
                            for kt in range(qb + 1):
                                n = i * (qb + 1) + kt
                                last = nc.tensor.transpose(out[:, n * P:(n + 1) * P],
                                                           probs[:, (done + u) % 3, i, kt * P:(kt + 1) * P], ident)
                        last.then_inc(a_full, 1)
                        turned[u] = made.now(a_full)

                    turned = {}

                    def values(u):
                        pe.wait_ge(a_free, turned[u])
                        pt = probs_t[:, (done + u) % 2, :]
                        if u < 2:
                            if u == 0:
                                opened[0] = bank_v()
                            out = opened[0]
                            for i in range(2):
                                for kt in range(qb + 1):
                                    n = i * (qb + 1) + kt
                                    v = AV + (2 * i + u) * HD
                                    last = part(out[u * HD:(u + 1) * HD, i * P:(i + 1) * P], tokens[:, kt, v:v + HD],
                                                pt[:, n * P:(n + 1) * P], start=(i == 0 and kt == 0), stop=(kt == qb))
                            last.then_inc(pv_done, 1)
                            return
                        g, kv = (u - 2) // 2, (u - 2) % 2
                        if kv == 0:
                            opened[0] = bank_v()
                            part(opened[0][:, 0:P], vcmp[0:HD, g * P:(g + 1) * P], pc_t[0:HD, :], start=True, stop=False)
                        out = opened[0]
                        for i, base in enumerate((BS, BW)):
                            for kt in range(qb + 1):
                                n = i * (qb + 1) + kt
                                v = base + P + kv * HD
                                last = part(out[kv * HD:(kv + 1) * HD, 0:P], tokens[:, kt, v:v + HD],
                                            pt[:, n * P:(n + 1) * P], start=False, stop=(i == 1 and kt == qb))
                        last.then_inc(pv_done, 1)

                    for k in range(0 if ua else 2):
                        out = bank_s()
                        for g in range(4):
                            last = part(out[:, g * 8:g * 8 + 8], feats[k * HD:(k + 1) * HD, 4 + g, q_cols],
                                        kcmp[k * HD:(k + 1) * HD, :], start=(g == 0), stop=(g == 3))
                        last.then_inc(s_full, 1)
                    scores(ua)
                    scores(ua + 1)
                    if ua == 0:
                        pe.wait_ge(probs_ready, done + 1 + (2 * l + qb))
                        out = bank_a()
                        nc.tensor.transpose(out[0:HD, 0:P], pc[:, :], ident).then_inc(a_full, 1)
                    for u in range(ua, ub):
                        if u + 2 < ub:
                            scores(u + 2)
                        turn(u)
                        if u > ua:
                            values(u - 1)
                    values(ub - 1)

            def sample_scores(l, hf):
                n = 2 * l + hf
                pe.wait_ge(q_ready, n + 1)
                pe.wait_ge(gates_ready, 3 * (l + 1))
                if hf:
                    pe.wait_ge(s_free, made.now(s_full))
                b0 = SEQ + hf * HALF

                def qb_(b):
                    return q_b[:, b * RB:(b + 1) * RB]

                def qa_(b, c):
                    return q_a[:, (b * 2 + c) * RA:(b * 2 + c + 1) * RA]

                out = bank_v()
                for b in range(HALF):
                    k0 = (hf * HALF + b) * CMP
                    part(out[0:RB, 0:CMP], qb_(b), kcmp_s[:, k0:k0 + CMP], start=(b == 0), stop=False)
                for b in range(HALF):
                    for i in range(2):
                        part(out[0:RB, CMP + i:CMP + 1 + i], qb_(b), feats[:, 8 + i, b0 + b:b0 + b + 1], start=False, stop=False)
                    for c in range(2):
                        last = part(out[0:RA, CMP + 2:CMP + 3], qa_(b, c), feats[:, 2 + c, b0 + b:b0 + b + 1],
                                    start=False, stop=False)
                last.then_inc(v_full, 1)
                out = bank_v()
                ex = table_of("expand", DEC).rearrange("p (h r) -> p h r", h=2)
                mm(out[0:RB, 0:N_GATES], ex[:, hf, :], gates[0:DEC, 2, :], start=True, stop=True).then_inc(v_full, 1)
                pending = []

                def multiply(b, i, m, tile):
                    pe.wait_ge(a_free if i % 2 else v_free, tile)
                    kt = key_t[:, m % 4, :]
                    if i < 3:
                        last = part(banks[5 + i][0:RB, :], qb_(b), kt, start=(b == 0), stop=(b == HALF - 1))
                    else:
                        for c in range(2):
                            last = part(banks[4][0:RA, 0:256], qa_(b, c), kt[:, c * 256:(c + 1) * 256],
                                        start=(b == 0 and c == 0), stop=(b == HALF - 1 and c == 1))
                    last.then_inc(kt_used, 1)

                for b in range(HALF):
                    s = b
                    pe.wait_ge(ring_in[s], 16 * 12 * (n + 1))
                    for i in range(4):
                        m = (n * HALF + b) * 4 + i
                        out = bank_a() if i % 2 else bank_v()
                        for j in range(4):
                            if i < 3:
                                src = ring[:, s, (4 * i + j) * 256:(4 * i + j) * 256 + P]
                            else:
                                c, kt = j // 2, j % 2
                                src = ring[:, s, 3072 + kt * 512 + c * P:3072 + kt * 512 + (c + 1) * P]
                            last = nc.tensor.transpose(out[:, j * P:(j + 1) * P], src, ident)
                        last.then_inc(a_full if i % 2 else v_full, 1)
                        pending.append((b, i, m, made.now(a_full if i % 2 else "v tiles")))
                        if len(pending) > 2:
                            multiply(*pending.pop(0))
                    if b == 0:
                        pe.wait_ge(imp_ready, n + 1)
                        out = bank_v()
                        mm(out[0:RB, 0:CMP], table_of("same", RB), s_cmp[0:RB, :], start=True, stop=True).then_inc(v_full, 1)
                while pending:
                    multiply(*pending.pop(0))

            def sample_values(l, hf):
                n = 2 * l + hf
                pe.wait_ge(s_probs, n + 1)
                out = bank_v()
                idb, ida = ident[0:RB, 0:RB], ident[0:RA, 0:RA]
                for t in range(12):
                    src = s_sel[0:RB, t * P:(t + 1) * P] if t < 8 else s_win[0:RB, (t - 8) * P:(t - 7) * P]
                    nc.tensor.transpose(out[:, t * RB:(t + 1) * RB], src, idb)
                nc.tensor.transpose(out[:, 480:512], s_cmp4[0:RB, :], idb)
                nc.tensor.transpose(out[0:DEC, 384:416], own_p[0:RB, 0:8], idb)
                nc.tensor.transpose(out[0:DEC, 416:448], own_p[0:RB, 8:16], idb).then_inc(v_full, 1)
                out = bank_v()
                for t in range(2):
                    nc.tensor.transpose(out[:, t * RA:(t + 1) * RA], s_a[0:RA, t * P:(t + 1) * P], ida)
                nc.tensor.transpose(out[0:DEC, 2 * RA:3 * RA], own_p[0:RA, 16:24], ida).then_inc(v_full, 1)
                pe.wait_ge(s_pt, n + 1)
                out_b, out_a = bank_v(), bank_v()
                for b in range(HALF):
                    rows8, cols = slice(b * 8, b * 8 + 8), slice(b * P, (b + 1) * P)
                    part(out_b[0:8, cols], p_t[0:DEC, 384:416][:, rows8], samples[:, BS + P:BS + 2 * P], start=(b == 0), stop=False)
                    part(out_b[0:8, cols], p_t[0:DEC, 416:448][:, rows8], samples[:, BW + P:BW + 2 * P], start=False, stop=False)
                    part(out_b[0:8, cols], p_t[:, 480:512][:, rows8], vcmp_s[:, hf * P:(hf + 1) * P], start=False, stop=False)
                    for t in range(12):
                        part(out_b[0:8, cols], p_t[:, t * RB:(t + 1) * RB][:, rows8], ring[:, b, t * 256 + P:(t + 1) * 256],
                             start=False, stop=(t == 11))
                    for c in range(2):
                        two = slice(b * 4 + 2 * c, b * 4 + 2 * c + 2)
                        out = out_a[c * 32:c * 32 + 2, cols]
                        part(out, p_t[0:DEC, 512 + 2 * RA:512 + 3 * RA][:, two], samples[:, AV + c * P:AV + (c + 1) * P],
                             start=(b == 0), stop=False)
                        for kt in range(2):
                            last = part(out, p_t[:, 512 + kt * RA:512 + (kt + 1) * RA][:, two],
                                        ring[:, b, 3328 + kt * 512 + c * P:3328 + kt * 512 + (c + 1) * P],
                                        start=False, stop=(kt == 1))
                    last.then_inc(ring_used, 1)
                pe.wait_ge(outs_ready, n + 1)
                out = bank_v()
                for b in range(HALF):
                    cols = slice(b * P, (b + 1) * P)
                    nc.tensor.transpose(out[:, b * 8:b * 8 + 8], outs[0:8, 0, cols], ident[0:8, 0:8])
                    for c in range(2):
                        o = RB + c * RA + b * 4 + 2 * c
                        last = nc.tensor.transpose(out[:, o:o + 2], outs[0:2, 1 + c, cols], ident[0:2, 0:2])
                last.then_inc(v_full, 1)

            def squares_ffn(g):
                return squares[:, g % 2, :]

            for l in range(DEPTH):
                ffn(l, 0, 0)
                mix(l)
                ffn(l, 1, WOUT_USE + 2)
            wait_x(DEPTH, 0)
            for t in range(3):
                r, col, _ = rows_of(t)
                for half in range(2):
                    out = bank_v()
                    for c in range(4):
                        last = nc.tensor.transpose(out[0:r, c * P:(c + 1) * P], x[:, half * 4 + c, col], ident)
                    last.then_inc(v_full, 1)

        @block.scalar
        def _(act):
            made = Tally()
            go = nc.scalar.activation
            act.wait_ge(warm_ready, 1)

            def bank_a():
                n = made.next(a_full)
                act.wait_ge(a_full, n)
                return banks[2 + (n - 1) % 2]

            def own():
                act.wait_ge(act_own, made.now(act_own))

            def mark(ins):
                made.next(act_own)
                return ins.then_inc(act_own, 1)

            def square_chunks(n):
                go(warm[:, :], warm[:, :], ACT.Sqrt)
                for g in range(KC):
                    act.wait_ge(z_done, n * KC + g + 1)
                    if n * KC + g >= 2:
                        act.wait_ge(stat_done, n * KC + g - 1)
                    go(squares[:, g % 2, :], z[:, g, :], ACT.Square).then_inc(sq_done, 1)
                norm(n)

            def norm(n):
                l, i = n // 3, n % 3
                act.wait_ge(stat_done, (n + 1) * KC)
                act.wait_ge(mean_done, n + 1)
                go(rstd[:, 1, :], mean_sb[:, :], ACT.Square).then_inc(musq_done, 1)
                act.wait_ge(var_done, n + 2)
                go(rstd[:, 0, :], rstd[:, 0, :], ACT.Sqrt).then_inc(std_done, 1)
                for c in range(KC):
                    act.wait_ge(norm_done, n * KC + c + 1)
                    go(x[:, c, :], z[:, c, :], ACT.Identity, bias=params[:, l, 24 + i * 8 + c:25 + i * 8 + c],
                       scale=params[:, l, i * 8 + c:i * 8 + c + 1]).then_inc(x_ready, 1)
                if i != 0 and n < 3 * DEPTH - 1:
                    go(warm[:, :], warm[:, :], ACT.Silu)

            def ffn(l, j):
                f = 2 * l + j

                def chunk(n, q, always):
                    act.wait_ge(gate_full, n + (f * FC + q + 1))
                    if always:
                        act.wait_ge(hidden_done, n + (f * FC + q - 1))
                    go(silu[:, q, :], banks[2 * q][:, 0:TOK], ACT.Silu).then_inc(silu_done, 1)

                for q in range(2):
                    chunk(0, q, f > 0)
                with act.Fori(1, FC // 2) as i:
                    for q in range(2):
                        chunk(i * 2, q, True)
                if f == 0:
                    act.wait_ge(var_done, 1)
                    go(rstd[:, 0, 0:4], rstd[:, 0, 0:4], ACT.Exp).then_inc(std_done, 1)
                square_chunks(3 * l + 2 * j)

            def mix(l):
                for c in range(2):
                    ps = bank_a()
                    go(gelu[:, c, :], ps[:, 0:TOK], ACT.Gelu_apprx_tanh).then_inc(a_free, 1)
                for c in range(2):
                    for i, dst in enumerate((lru_r, lru_i)):
                        ps = bank_a()
                        go(dst[:, c, :], ps[:, 0:TOK], ACT.Sigmoid,
                           bias=params[:, l, 66 + 2 * i + c:67 + 2 * i + c]).then_inc(a_free, 1)
                act.wait_ge(a_free, made.now(a_full))
                for c in range(2):
                    go(lru_t[:, c, :], lru_r[:, c, :], ACT.Tanh, scale=decay[:, l, c:c + 1]).then_inc(gate_r, 1)
                for c in range(2):
                    go(rstd[:, c, :], lru_r[:, c, :], ACT.Exp, scale=decay[:, l, c:c + 1]).then_inc(gate_r, 1)
                act.wait_ge(lru_f, l + 1)
                for c in range(2):
                    go(lru_t[:, c, :], lru_t[:, c, :], ACT.Sqrt, scale=-1.0).then_inc(lru_s, 1)
                act.wait_ge(gates_raw, l + 1)
                for t in range(3):
                    r, _, _ = rows_of(t)
                    go(gates[0:r, t, :], gates[0:r, t, :], ACT.Sigmoid).then_inc(gates_ready, 1)
                for n in range(0, 10, 2):
                    ps = bank_a()
                    go(feats[:, n, :], ps[:, 0:TOK], ACT.Copy).then_inc(a_free, 1)
                sample_scores(l, 0)
                prompt_block(l, 0, 0, 10)
                prompt_block(l, 1, 0, SPLIT)
                sample_scores(l, 1)
                prompt_block(l, 1, SPLIT, 10)
                act.wait_ge(mix_ready, l + 1)
                for c in range(KC):
                    if c >= 2:
                        act.wait_ge(rms_stat, l * KC + c - 1)
                    go(squares[:, c % 2, :], mixed[:, c, :], ACT.Square).then_inc(rms_sq, 1)
                act.wait_ge(rms_stat, (l + 1) * KC)
                for g, widths in enumerate((4.0, 2.0, 4.0)):
                    go(rstd[:, g, :], banks[4 + g][:, 0:TOK], ACT.Sqrt, bias=eps[:, 1:2], scale=widths).then_inc(rms_std, 1)
                square_chunks(3 * l + 1)

            def prompt_block(l, qb, ua, ub):
                nk = (qb + 1) * P
                done = (2 * l + qb) * 10
                if ua == 0:
                    act.wait_ge(masked, done + (2 * l + qb) + 1)
                    go(pc[:, :], pc[:, :], ACT.Exp).then_inc(exps, 1)

                def exp_unit(u):
                    act.wait_ge(masked, done + (2 * l + qb) + 2 + u)
                    r = (done + u) % 3
                    for i in range(2):
                        last = go(probs[:, r, i, 0:nk], probs[:, r, i, 0:nk], ACT.Exp, scale=-1.0,
                                  bias=stat[:, (done + u) % 4, i:i + 1],
                                  accum_out=stat[:, (done + u) % 4, 2 + i:3 + i])
                    last.then_inc(exps, 1)

                def evac(u):
                    if done + u >= 2:
                        act.wait_ge(pv_done, done + u - 1)
                    ps = bank_a()
                    n = 2 * (qb + 1) * P
                    go(probs_t[:, (done + u) % 2, 0:n], ps[:, 0:n], ACT.Copy).then_inc(a_free, 1)

                exp_unit(ua)
                if ua == 0:
                    if qb or l:
                        act.wait_ge(pv_done, done)
                    ps = bank_a()
                    go(pc_t[0:HD, :], ps[0:HD, 0:P], ACT.Copy).then_inc(a_free, 1)
                for u in range(ua + 1, ub):
                    exp_unit(u)
                    evac(u - 1)
                evac(ub - 1)

            def sample_scores(l, hf):
                n = 2 * l + hf

                def exp_rows(k, s_, rows_):
                    act.wait_ge(s_masked, 4 * n + k + 1)
                    go(s_[0:rows_, :], s_[0:rows_, :], ACT.Exp, scale=-1.0, bias=s_stat[0:rows_, k:k + 1],
                       accum_out=s_stat[0:rows_, 8 + k:9 + k]).then_inc(s_exps, 1)

                exp_rows(0, s_cmp, RB)
                for b in range(HALF):
                    for i in (1, 3):
                        m = (n * HALF + b) * 4 + i
                        if m >= 4:
                            act.wait_ge(kt_used, m - 3)
                        ps = bank_a()
                        go(key_t[:, m % 4, :], ps[:, :], ACT.Copy).then_inc(a_free, 1)
                exp_rows(1, s_sel, RB)
                exp_rows(2, s_win, RB)
                exp_rows(3, s_a, RA)

            for l in range(DEPTH):
                ffn(l, 0)
                mix(l)
                ffn(l, 1)

        @block.vector
        def _(dve):
            made = Tally()
            ttr = nc.vector.tensor_tensor_reduce
            tt, ts, stt, copy = nc.vector.tensor_tensor, nc.vector.tensor_scalar, nc.vector.scalar_tensor_tensor, nc.vector.tensor_copy
            reduce = nc.vector.tensor_reduce

            def bank_v(full=v_full, value=None):
                n = made.next("v tiles")
                dve.wait_ge(full, made.next(v_full) if value is None else value)
                return banks[(n - 1) % 2]

            def free_v(ins):
                ins.then_inc(v_free, 1)

            def v_read():
                dve.wait_ge(v_free, made.now("v tiles"))

            def step(ins):
                ins.then_inc(vec, 1)
                dve.wait_ge(vec, made.next(vec))

            def mark(ins):
                ins.then_inc(vec, 1)
                made.next(vec)

            def settle():
                dve.wait_ge(vec, made.now(vec))

            mark(nc.vector.memset(eps[:, 0:1], EPS / ALPHA ** 2))
            mark(nc.vector.memset(eps[:, 1:2], EPS))
            for c in range(KC):
                ps = bank_v()
                free_v(copy(x[:, c, :], ps[:, 0:TOK]))
            v_read()
            dve.sem_inc(x_ready, KC)
            def columns():
                for l in range(DEPTH):
                    ps = bank_v()
                    copy(params[:, l, :], ps[:, 0:72])
                    free_v(copy(states[:, l, :], ps[:, 128:192]))
                v_read()
                lam = params[:, :, 70:72]
                e = rstd[:, 0, 0:4].rearrange("p (l c) -> p l c", l=2)
                s1, s2, s3 = (rstd[:, 1, 4 * i:4 * i + 4].rearrange("p (l c) -> p l c", l=2) for i in range(3))
                step(ts(s1, lam, -1.0, None, ALU.mult))
                tt(e, lam, s1, ALU.min).then_inc(var_done, 1)
                dve.wait_ge(std_done, 1)
                step(ts(s2, e, 2.0, None, ALU.add))
                step(nc.vector.reciprocal(s2, s2))
                step(tt(e, e, s2, ALU.mult))
                step(tt(s2, e, e, ALU.mult))
                step(ts(s3, s2, 1.0 / 15, 1.0 / 13, ALU.mult, ALU.add))
                for odd in (11, 9, 7, 5, 3, 1):
                    step(tt(s3, s3, s2, ALU.mult))
                    step(ts(s3, s3, 1.0 / odd, None, ALU.add))
                step(tt(s3, s3, e, ALU.mult))
                step(ts(s1, s1, 0.0, None, ALU.max))
                step(stt(s3, s3, 2.0, s1, ALU.mult, ALU.add))
                step(ts(decay[:, :, :], s3, -LRU_C, None, ALU.mult))

            def residual(n, factor):
                for g in range(KC):
                    dve.wait_ge(y_full, n * KC + g + 1)
                    stt(z[:, g, :], banks[4 + g % 2][:, 0:TOK], factor, x[:, g, :], ALU.mult, ALU.add).then_inc(z_done, 1)
                dve.wait_ge(stat_done, (n + 1) * KC)
                copy(mean_sb[:, :], banks[6][:, 0:TOK]).then_inc(mean_done, 1)
                v = rstd[:, 0, :]
                dve.wait_ge(musq_done, n + 1)
                step(tt(v, banks[7][:, 0:TOK], rstd[:, 1, :], ALU.subtract))
                ts(v, v, 0.0, eps[:, 0:1], ALU.max, ALU.add).then_inc(var_done, 1)
                dve.wait_ge(std_done, n + 2)
                step(nc.vector.reciprocal(v, v))
                for c in range(KC):
                    dve.wait_ge(sub_done, n * KC + c + 1)
                    tt(z[:, c, :], z[:, c, :], v, ALU.mult).then_inc(norm_done, 1)

            def ffn(l, j):
                f = 2 * l + j

                def chunk(n, q, out):
                    dve.wait_ge(silu_done, n + (f * FC + q + 1))
                    dve.wait_ge(up_full, n + (f * FC + q + 1))
                    tt(out, silu[:, q, :], banks[2 * q + 1][:, 0:TOK], ALU.mult).then_inc(hidden_done, 1)

                if f:
                    dve.wait_ge(rows_stored, 16 * 8 * (l + j))
                    dve.wait_ge(states_stored, 16 * 4 * (l + j))
                with dve.Fori(0, FC // 2) as i:
                    for q in range(2):
                        chunk(i * 2, q, hidden[:, bass.ds(i * 2 + q, 1), :].rearrange("p c t -> p (c t)"))
                if f == 0:
                    columns()
                residual(3 * l + 2 * j, 0.5 / ALPHA)

            def rope(ps, col, heads, dst, t, r):
                cos = table_of("cos", r)[:, t * HD:(t + 1) * HD].unsqueeze(1)
                sin = table_of("sin", r)[:, t * HD:(t + 1) * HD].unsqueeze(1)
                src = ps[0:r, col:col + heads * HD].rearrange("p (h d) -> p h d", h=heads)
                t1 = rope_t[0:r, 0, 0:heads * HD].rearrange("p (h d) -> p h d", h=heads)
                t2 = rope_t[0:r, 1, 0:heads * HD].rearrange("p (h d) -> p h d", h=heads)
                hf = HD // 2
                tt(t1, src, cos.to_broadcast([r, heads, HD]), ALU.mult)
                tt(t2[:, :, 0:hf], src[:, :, hf:HD], sin[:, :, 0:hf].to_broadcast([r, heads, hf]), ALU.mult)
                step(tt(t2[:, :, hf:HD], src[:, :, 0:hf], sin[:, :, hf:HD].to_broadcast([r, heads, hf]), ALU.mult))
                return tt(dst, t1, t2, ALU.add)

            def mix(l):
                par = params[:, l, :]
                if l == 0:
                    dve.wait_ge(small_in, 16 * 17 * DEPTH)
                weighted = [0]

                def weight():
                    k = l * 2 * DEC + weighted[0]
                    weighted[0] += 1
                    dve.wait_ge(bc_in[k % 2], 64 * (k // 2 + 1))
                    pages = bc_pages[:, k % 2, :, :]
                    tt(pages, pages, cmp_w[:, l, :].unsqueeze(1).to_broadcast([P, 4, 256]), ALU.mult).then_inc(bc_weighted, 1)

                mark(nc.vector.memset(conv_x[:, :, 0:3], 0.0))
                for c in range(2):
                    ps = bank_v()
                    copy(conv_x[:, c, 3:259], ps[:, 0:SEQ])
                    copy(conv_s[:, c, :, 0:3], states[:, l, c * 24:c * 24 + 24].rearrange("p (b j) -> p b j", b=DEC))
                    free_v(copy(conv_s[:, c, :, 3], ps[:, SEQ:TOK]))
                v_read()
                for c in range(2):
                    for j in range(4):
                        wj = par[:, 56 + 2 * j + c:57 + 2 * j + c]
                        for dst, src in ((xc[:, c, 0:SEQ], conv_x[:, c, j:j + SEQ]), (xc[:, c, SEQ:TOK], conv_s[:, c, :, j])):
                            if j == 0:
                                mark(ts(dst, src, wj, par[:, 64 + c:65 + c], ALU.mult, ALU.add))
                            else:
                                mark(stt(dst, src, wj, dst, ALU.mult, ALU.add))
                        settle()
                dve.sem_inc(xc_ready, 1)
                for g in range(4):
                    for t in range(3):
                        r, _, tok = rows_of(t)
                        weight()
                        ps = bank_v()
                        heads = lambda a, n: tok[:, a:a + n * HD].rearrange("p (h d) -> p h d", h=n)
                        bq = tok[:, BQ:BQ + 512].rearrange("p (g k d) -> p g k d", g=4, k=2)
                        if g == 0:
                            last = rope(ps, 0, 8, heads(AQ, 8), t, r)
                        elif g == 1:
                            rope(ps, 256, 4, bq[:, :, 0, :], t, r)
                            last = copy(tok[:, AV:AV + 256], ps[0:r, 0:256])
                        elif g == 2:
                            mark(rope(ps, 0, 4, bq[:, :, 1, :], t, r))
                            settle()
                            rope(ps, 256, 2, heads(BC, 2), t, r)
                            last = copy(tok[:, BC + P:BC + 2 * P], ps[0:r, 384:512])
                        else:
                            mark(rope(ps, 0, 2, heads(BS, 2), t, r))
                            settle()
                            rope(ps, 256, 2, heads(BW, 2), t, r)
                            copy(tok[:, BS + P:BS + 2 * P], ps[0:r, P:2 * P])
                            last = copy(tok[:, BW + P:BW + 2 * P], ps[0:r, 384:512])
                        free_v(last)
                        v_read()
                        dve.sem_inc(tok_ready, 1)
                    if g == 0:
                        dve.wait_ge(gate_r, 4 * (l + 1))
                        a, th = rstd[:, 0:2, :], lru_t
                        ix = xc
                        mark(tt(lru_r[:, :, :], a, a, ALU.mult))
                        step(tt(ix[:, :, :], lru_i[:, :, :], xc[:, :, :], ALU.mult))
                        step(stt(th, lru_r[:, :, :], 1.0, th, ALU.add, ALU.mult))
                        dve.sem_inc(lru_f, 1)
                    if g == 1:
                        dve.wait_ge(lru_s, 2 * (l + 1))
                        step(tt(ix, th, ix, ALU.mult))
                        hs = lru_r
                        for c in range(2):
                            mark(nc.vector.tensor_tensor_scan(hs[:, c, 0:SEQ], a[:, c, 0:SEQ], ix[:, c, 0:SEQ], 0.0, ALU.mult, ALU.add))
                        h0 = states[:, l, 48:64].rearrange("p (c b) -> p c b", c=2)
                        step(tt(hs[:, :, SEQ:TOK], a[:, :, SEQ:TOK], h0, ALU.mult))
                        step(tt(hs[:, :, SEQ:TOK], hs[:, :, SEQ:TOK], ix[:, :, SEQ:TOK], ALU.add))
                        for c in range(2):
                            copy(finals[:, c, 0:1], hs[:, c, SEQ - 1:SEQ])
                            copy(finals[:, c, 1:9], hs[:, c, SEQ:TOK])
                            copy(finals[:, c, 9:12], conv_x[:, c, SEQ:SEQ + 3])
                            mark(copy(finals[:, c, 12:36].rearrange("p (b j) -> p b j", b=DEC), conv_s[:, c, :, 1:4]))
                        settle()
                        dve.sem_inc(finals_ready, 1)
                        mark(tt(mixed[:, 6:8, :], hs, gelu, ALU.mult))
                    if g == 2:
                        weight()
                        ps = bank_v()
                        free_v(copy(finals_t[0:36, :], ps[0:36, 0:256]))
                        v_read()
                        dve.sem_inc(state_ready, 1)
                for t in range(3):
                    r, _, _ = rows_of(t)
                    weight()
                    ps = bank_v()
                    free_v(tt(gates[0:r, t, :], ps[0:r, 0:N_GATES], gate_bias[0:r, l, :], ALU.add))
                v_read()
                dve.sem_inc(gates_raw, 1)
                for n in range(1, 10, 2):
                    ps = bank_v()
                    free_v(copy(feats[:, n, :], ps[:, 0:TOK]))
                prompt_start(l)
                sample_scores(l, 0)
                prompt_block(l, 0, 0, 10)
                sample_values(l, 0)
                prompt_block(l, 1, 0, SPLIT)
                sample_scores(l, 1)
                prompt_block(l, 1, SPLIT, 10)
                sample_values(l, 1)
                v_read()
                dve.sem_inc(mix_ready, 1)
                for g in range(3):
                    dve.wait_ge(rms_std, 3 * l + g + 1)
                    mark(nc.vector.reciprocal(rstd[:, g, :], rstd[:, g, :]))
                settle()
                for c in range(KC):
                    g = 0 if c < 2 else 1 if c < 6 else 2
                    stt(mixed[:, c, :], mixed[:, c, :], par[:, 48 + c:49 + c], rstd[:, g, :], ALU.mult, ALU.mult)\
                        .then_inc(yn_ready, 1)
                dve.wait_ge(rows_stored, 16 * 8 * (l + 1))
                residual(3 * l + 1, 1.0 / ALPHA)

            n_s = [0]

            def bank_s():
                n_s[0] += 1
                dve.wait_ge(s_full, n_s[0])
                return banks[5 + (n_s[0] - 1) % 3]

            def prompt_start(l):
                settle()
                for t in range(TT):
                    mark(tt(prod_c[:, t, 0:256], tokens[:, t, BC:BC + 256], cmp_w[:, l, :], ALU.mult))
                settle()
                dve.sem_inc(prod_ready, 1)
                ps = bank_v()
                copy(kcmp[:, :], ps[:, 0:8])
                free_v(tt(vcmp[0:HD, :].rearrange("p (g n) -> p g n", g=4),
                          ps[0:HD, P:2 * P].unsqueeze(1).to_broadcast([HD, 4, P]),
                          table_of("maskv", HD).rearrange("p (g n) -> p g n", g=4), ALU.mult))
                v_read()
                dve.sem_inc(cmp_ready, 1)
                dve.wait_ge(gates_ready, 3 * (l + 1))
                dve.wait_ge(a_full, l * A_LAYER + 11)
                dve.wait_ge(bc_used, (l + 1) * 2 * DEC)
                both = banks[4][:, :].rearrange("p (h w n) -> p h w n", h=2, w=2)
                copy(vcmp_s.rearrange("p (h n) -> p h n", h=2), both[:, :, 1, :])
                copy(kcmp_rows, both[:, :, 0, :]).then_inc(cmp_out, 1)
                ps = bank_v()
                free_v(copy(kcmp_s, ps[:, 0:2 * P]))
                v_read()

            def prompt_block(l, qb, ua, ub):
                    nk = (qb + 1) * P
                    done = (2 * l + qb) * 10
                    p3 = pc[:, :].rearrange("p (h n) -> p h n", h=8)
                    vis_add = table_of("vis_add")[:, qb * 8:qb * 8 + 8].unsqueeze(1).to_broadcast([P, 8, 8])
                    vis = table_of("vis")[:, qb * 8:qb * 8 + 8].unsqueeze(1).to_broadcast([P, 8, 8])
                    mx, sm, gt = pc_stat[:, 0:8], pc_stat[:, 8:16], pc_stat[:, 16:24]
                    if ua == 0:
                        for k in range(2):
                            ps = bank_s()
                            stt(pc[:, :].rearrange("p (g k n) -> p g k n", g=4, k=2)[:, :, k, :],
                                ps[:, 0:32].rearrange("p (g n) -> p g n", g=4), SCALE, vis_add[:, 0:4, :],
                                ALU.mult, ALU.add).then_inc(s_free, 1)
                        dve.wait_ge(s_free, n_s[0])
                        step(reduce(mx, p3, AX_X, ALU.max))
                        tt(p3, p3, mx.unsqueeze(2).to_broadcast([P, 8, 8]), ALU.subtract).then_inc(masked, 1)

                    def mask_unit(u):
                        ps = bank_s()[:, :].rearrange("p (b n) -> p b n", b=2)[:, :, 0:nk]
                        m = table_of("mask_a" if u < 2 else "mask_c")[:, qb * SEQ:qb * SEQ + nk]
                        r = (done + u) % 3
                        for i in range(2):
                            ttr(probs[:, r, i, 0:nk], ps[:, i, :], m, -SCALE, -MASKED, ALU.add, ALU.min,
                                stat[:, (done + u) % 4, i:i + 1]).then_inc(masked if i else s_free, 1)

                    def norm_unit(u):
                        dve.wait_ge(exps, done + (2 * l + qb) + 2 + u)
                        st = stat[:, (done + u) % 4, :]
                        step(nc.vector.reciprocal(st[:, 4:6], st[:, 2:4]))
                        if u >= 2:
                            h = ((u - 2) % 2) * 4 + (u - 2) // 2
                            step(tt(st[:, 4:6], st[:, 4:6], gates[:, qb, 3 * h + 1:3 * h + 3], ALU.mult))
                        pr = probs[:, (done + u) % 3, :, 0:nk]
                        tt(pr, pr, st[:, 4:6].unsqueeze(2).to_broadcast([P, 2, nk]), ALU.mult).then_inc(probs_ready, 1)

                    def collect(u):
                        if u < 0 or u % 2 == 0:
                            return
                        c = 2 + (u - 2) // 2
                        ps = bank_v(pv_done, done + u + 1)
                        if u == 1:
                            free_v(copy(mixed[:, 0:2, qb * P:(qb + 1) * P], ps[:, 0:2 * P].rearrange("p (c q) -> p c q", c=2)))
                            return
                        free_v(copy(mixed[:, c, qb * P:(qb + 1) * P], ps[:, 0:P]))

                    mask_unit(ua)
                    if ua == 0:
                        dve.wait_ge(exps, done + (2 * l + qb) + 1)
                        step(tt(p3, p3, vis, ALU.mult))
                        step(reduce(sm, p3, AX_X, ALU.add))
                        step(ts(sm, sm, 1e-30, None, ALU.max))
                        step(nc.vector.reciprocal(sm, sm))
                        gate0 = gates[:, qb, :].rearrange("p (k g t) -> p g k t", k=2, g=4)[:, :, :, 0]
                        step(tt(gt.rearrange("p (g k) -> p g k", k=2), sm.rearrange("p (g k) -> p g k", k=2), gate0, ALU.mult))
                        tt(p3, p3, gt.unsqueeze(2).to_broadcast([P, 8, 8]), ALU.mult).then_inc(probs_ready, 1)
                    for u in range(ua + 1, ub):
                        mask_unit(u)
                        norm_unit(u - 1)
                        if u - 3 >= ua:
                            collect(u - 3)
                    norm_unit(ub - 1)
                    for u in range(ub - 3, ub):
                        collect(u)

            def sample_scores(l, hf):
                n = 2 * l + hf
                b0 = SEQ + hf * HALF
                if hf == 0:
                    step(nc.vector.memset(q_b, 0.0))
                    step(nc.vector.memset(q_a, 0.0))
                for k in range(2):
                    half = slice(k * HD, (k + 1) * HD)
                    mark(copy(q_b[half, :].rearrange("p (b k) -> p b k", k=40)[:, :, k:k + 8:2],
                              feats[half, 4:8, b0:b0 + HALF].rearrange("p g b -> p b g")))
                    mark(copy(q_a[half, :].rearrange("p (b c k) -> p b c k", c=2, k=18)[:, :, :, k],
                              feats[half, 0:2, b0:b0 + HALF].rearrange("p c b -> p b c")))
                settle()
                dve.sem_inc(q_ready, 1)
                st = s_stat[0:RB, :]
                ps = bank_v()
                mark(ts(s_cmp[0:RB, :], ps[0:RB, 0:CMP], -SCALE, None, ALU.mult))
                mark(ts(s_sel[0:RB, 1024:1025], ps[0:RB, CMP:CMP + 1], -SCALE, None, ALU.mult))
                mark(ts(s_win[0:RB, 512:513], ps[0:RB, CMP + 1:CMP + 2], -SCALE, None, ALU.mult))
                free_v(ts(s_a[0:RA, 256:257], ps[0:RA, CMP + 2:CMP + 3], -SCALE, -LOG_OWN, ALU.mult, ALU.add))
                v_read()
                reduce(st[:, 0:1], s_cmp[0:RB, :], AX_X, ALU.min).then_inc(s_masked, 1)
                ps = bank_v()
                free_v(tt(st[:, 16:40], ps[0:RB, 0:N_GATES], table_of("headmask", RB), ALU.mult))
                v_read()
                mark(reduce(st[:, 40:43], st[:, 16:40].rearrange("p (h t) -> p t h", t=3), AX_X, ALU.add))

                def keys(b):
                    for i in (0, 2):
                        m = (n * HALF + b) * 4 + i
                        if m >= 4:
                            dve.wait_ge(kt_used, m - 3)
                        ps = bank_v()
                        free_v(copy(key_t[:, m % 4, :], ps[:, :]))

                dve.wait_ge(s_exps, 4 * n + 1)
                step(nc.vector.reciprocal(st[:, 12:13], st[:, 8:9]))
                step(ts(s_cmp[0:RB, :], s_cmp[0:RB, :], st[:, 12:13], None, ALU.mult))
                dve.sem_inc(imp_ready, 1)
                keys(0)
                step(ts(st[:, 44:48], table_of("own4", RB), st[:, 40:41], None, ALU.mult))
                mark(tt(s_cmp4[0:RB, :].rearrange("p (b n) -> p b n", b=HALF),
                        s_cmp[0:RB, :].unsqueeze(1).to_broadcast([RB, HALF, CMP]),
                        st[:, 44:48].unsqueeze(2).to_broadcast([RB, HALF, CMP]), ALU.mult))
                settle()
                ps = bank_v()
                imp, drop = st[:, 44:60], st[:, 60:76]
                free_v(reduce(imp, ps[0:RB, 0:CMP].rearrange("p (n t) -> p n t", t=2), AX_X, ALU.add))
                v_read()
                index = table_of("index", RB)
                step(reduce(st[:, 76:77], imp[:, 1:15], AX_X, ALU.min))
                step(nc.vector.memset(drop, 0.0))
                step(ts(drop[:, 1:15], imp[:, 1:15], st[:, 76:77], None, ALU.is_equal))
                step(tt(drop[:, 1:15], drop[:, 1:15], index, ALU.mult))
                step(reduce(st[:, 77:78], drop[:, 1:15], AX_X, ALU.max))
                step(ts(drop[:, 1:15], index, st[:, 77:78], MASKED, ALU.is_equal, ALU.mult))
                for b in range(1, HALF):
                    keys(b)
                dve.wait_ge(kt_used, 4 * HALF * (n + 1))
                for i in range(2):
                    sel = s_sel[0:RB, i * 512:(i + 1) * 512]
                    mark(stt(sel.rearrange("p (n k) -> p n k", n=8), banks[5 + i][0:RB, :].rearrange("p (n k) -> p n k", n=8),
                             1.0, drop[:, i * 8:(i + 1) * 8].unsqueeze(2).to_broadcast([RB, 8, HD]), ALU.mult, ALU.add))
                settle()
                step(ts(s_sel[0:RB, 0:1024], s_sel[0:RB, 0:1024], -SCALE, None, ALU.mult))
                reduce(st[:, 1:2], s_sel[0:RB, :], AX_X, ALU.min).then_inc(s_masked, 1)
                step(ts(s_win[0:RB, 0:512], banks[7][0:RB, :], -SCALE, None, ALU.mult))
                reduce(st[:, 2:3], s_win[0:RB, :], AX_X, ALU.min).then_inc(s_masked, 1)
                step(stt(s_a[0:RA, 0:256], banks[4][0:RA, 0:256], -SCALE, table_of("log_a", RA)[:, 0:256],
                         ALU.mult, ALU.subtract))
                reduce(s_stat[0:RA, 3:4], s_a[0:RA, :], AX_X, ALU.min).then_inc(s_masked, 1)

            def sample_values(l, hf):
                n = 2 * l + hf
                b0 = SEQ + hf * HALF
                st = s_stat[0:RB, :]
                dve.wait_ge(s_exps, 4 * n + 4)
                mark(nc.vector.reciprocal(st[:, 13:15], st[:, 9:11]))
                mark(nc.vector.reciprocal(s_stat[0:RA, 15:16], s_stat[0:RA, 11:12]))
                settle()
                mark(ts(s_sel[0:RB, :], s_sel[0:RB, :], st[:, 13:14], st[:, 41:42], ALU.mult, ALU.mult))
                mark(ts(s_win[0:RB, :], s_win[0:RB, :], st[:, 14:15], st[:, 42:43], ALU.mult, ALU.mult))
                mark(ts(s_a[0:RA, :], s_a[0:RA, :], s_stat[0:RA, 15:16], None, ALU.mult))
                settle()
                mine = table_of("own", RB)[:, hf * 8:hf * 8 + 8]
                mine_a = table_of("own_a", RA)[:, hf * 8:hf * 8 + 8]
                mark(ts(own_p[0:RB, 0:8], mine, s_sel[0:RB, 1024:1025], None, ALU.mult))
                mark(ts(own_p[0:RB, 8:16], mine, s_win[0:RB, 512:513], None, ALU.mult))
                mark(ts(own_p[0:RA, 16:24], mine_a, s_a[0:RA, 256:257], None, ALU.mult))
                settle()
                dve.sem_inc(s_probs, 1)
                ps = bank_v()
                copy(p_t[:, 0:384], ps[:, 0:384])
                copy(p_t[:, 480:512], ps[:, 480:512])
                free_v(copy(p_t[0:DEC, 384:448], ps[0:DEC, 384:448]))
                ps = bank_v()
                copy(p_t[:, 512:512 + 2 * RA], ps[:, 0:2 * RA])
                free_v(copy(p_t[0:DEC, 512 + 2 * RA:512 + 3 * RA], ps[0:DEC, 2 * RA:3 * RA]))
                v_read()
                dve.sem_inc(s_pt, 1)
                ps = bank_v(ring_used, HALF * (n + 1))
                free_v(copy(outs[:, 0, :], ps[0:8, :]))
                ps = bank_v(ring_used, HALF * (n + 1))
                copy(outs[0:2, 1, :], ps[0:2, :])
                free_v(copy(outs[0:2, 2, :], ps[32:34, :]))
                v_read()
                dve.sem_inc(outs_ready, 1)
                ps = bank_v()
                for k in range(2):
                    half = slice(k * HD, (k + 1) * HD)
                    copy(mixed[half, 2:6, b0:b0 + HALF].rearrange("p g b -> p b g"),
                         ps[half, 0:RB].rearrange("p (b g k) -> p b g k", g=4, k=2)[:, :, :, k])
                    for c in range(2):
                        last = copy(mixed[half, c, b0:b0 + HALF],
                                    ps[half, RB + c * RA:RB + (c + 1) * RA].rearrange("p (b k) -> p b k", k=4)[:, :, 2 * c + k])
                free_v(last)

            for l in range(DEPTH):
                ffn(l, 0)
                mix(l)
                ffn(l, 1)
            for t in range(3):
                r, _, _ = rows_of(t)
                for half in range(2):
                    ps = bank_v()
                    free_v(copy(stage[0:r, t, half * 512:(half + 1) * 512], ps[0:r, :]))
                    v_read()
                    dve.sem_inc(stage_ready, 1)


_INS = ["x_prompt", "x_sample", "cache_a_kv", "cache_bc_kv", "cache_bs_kv", "cache_bw_kv", "state_c_h", "state_c_conv",
        "page_table", "w_in", "b_gate", "cmp_wk", "cmp_wv", "out_g_a", "out_g_b", "out_g_c", "conv_w", "conv_b",
        "lru_wr", "lru_br", "lru_wi", "lru_bi", "lru_lam", "w_out", "ln_g", "ln_b", "ffn_wg", "ffn_wu", "ffn_wd"]
_OUTS = [(1, 256, 1024), (8, 1, 1024), (2, 1, 256, 2, 4, 64), (2, 8, 1, 2, 4, 64),
         (2, 1, 2, 128, 2, 2, 64), (2, 8, 1, 2, 2, 64), (2, 1, 2, 128, 2, 2, 64), (2, 8, 1, 2, 2, 64),
         (2, 1, 256, 2, 2, 64), (2, 8, 1, 2, 2, 64), (2, 1, 256), (2, 8, 256), (2, 1, 3, 256), (2, 8, 3, 256)]


def shape_table():
    import numpy as np

    t = {n: np.zeros((P, b - a), np.float32) for n, (a, b) in TABLE.items()}
    p = np.arange(P)
    t["ident"][p, p] = 1.0
    t["mean"][:] = 1.0 / D_MODEL
    key = np.arange(SEQ)[None, :]
    for qb in range(2):
        q = (qb * P + p)[:, None]
        delta = q - key
        count = ((delta <= 128).astype(int) + (delta % 4 == 0) + (delta % 16 == 0)) * (delta >= 0)
        t["mask_a"][:, qb * SEQ:(qb + 1) * SEQ] = np.where(count > 0, np.log(np.maximum(count, 1)) / SCALE, MASKED)
        t["mask_c"][:, qb * SEQ:(qb + 1) * SEQ] = np.where(delta >= 0, 0.0, MASKED)
        vis = (np.arange(8) * CMP + CMP - 1)[None, :] <= q
        t["vis"][:, qb * 8:qb * 8 + 8] = vis
        t["vis_add"][:, qb * 8:qb * 8 + 8] = np.where(vis, 0.0, MASKED)
    half = HD // 2
    freq = (np.float32(10000.0) ** (-np.arange(half, dtype=np.float32) / np.float32(half))).astype(np.float32)
    for i, pos in enumerate((p, P + p, np.full(P, PAST))):
        ang = pos.astype(np.float32)[:, None] * freq[None, :]
        c, s = np.cos(ang), np.sin(ang)
        t["cos"][:, i * HD:(i + 1) * HD] = np.concatenate([c, c], 1)
        t["sin"][:, i * HD:(i + 1) * HD] = np.concatenate([-s, s], 1)
    t["sel4"][p, p // CMP] = 1.0
    t["selw"][p, 28 + p // CMP] = 1.0
    for tile in range(2):
        for h in range(8):
            t["selrep"][p, tile * HD + h * 8 + tile * 4 + p // CMP] = 1.0
    back = np.concatenate([P - p, 512 - 4 * np.arange(96), PAST - 16 * np.arange(32), [0]])
    count = (back <= 128).astype(int) + (back % 4 == 0) * (back <= 512) + (back % 16 == 0)
    t["log_a"][:] = np.log(count)[None, :]
    r = np.arange(RB)
    t["same"][:RB] = ((r[:, None] // 8 == r[None, :] // 8) & (r[:, None] % 2 == r[None, :] % 2))
    for hf in range(2):
        for b in range(DEC):
            t["expand"][b, hf * RB:(hf + 1) * RB] = (hf * HALF + r // 8) == b
            t["own"][:RB, hf * 8 + b] = (hf * HALF + r // 8) == b
            t["own_a"][:RA, hf * 8 + b] = (hf * HALF + np.arange(RA) // 4) == b
    t["own4"][r, r // 8] = 1.0
    for row in r:
        g, k = (row % 8) // 2, row % 2
        h = k * 4 + g
        t["headmask"][row, 3 * h:3 * h + 3] = 1.0
    t["index"][:] = np.arange(1, 15)[None, :]
    for hd in range(8):
        g, k = hd // 2, hd % 2
        t["maskv"][hd * 8:hd * 8 + 8, g * P + k * HD:g * P + (k + 1) * HD] = 1.0
    return np.concatenate([t[n] for n in TABLE], axis=1)


def kernel(**inputs):
    import numpy as _np
    import concourse.bacc as _bacc
    from concourse import mybir as _mybir
    from concourse.bass_utils import run_bass_kernel_spmd as _run

    nc = _bacc.Bacc("TRN2", target_bir_lowering=False, num_devices=1)
    arrays, args = {}, []
    for name in _INS + ["table"]:
        a = shape_table() if name == "table" else _np.ascontiguousarray(inputs[name])
        arrays[f"in_{name}_dram"] = a
        args.append(nc.dram_tensor(f"in_{name}_dram", a.shape, _mybir.dt.from_np(a.dtype), kind="ExternalInput").ap())
    for i, shape in enumerate(_OUTS):
        args.append(nc.dram_tensor(f"out_{i}_dram", shape, _mybir.dt.float32, kind="ExternalOutput").ap())
    build(nc, *args)
    r = _run(nc, [arrays], core_ids=[0])
    return tuple(r.results[0][f"out_{i}_dram"] for i in range(len(_OUTS)))
```
